# Optimizing a Trainium2 kernel written in Bass

```python
import jax, jax.numpy as jnp
from jax import lax
import numpy as np

D_MODEL = 1024
BATCH = 1
SEQ = 512
DEPTH = 2
DEC_BATCH = 1
DEC_SEQ = 64
PAST_LEN = 512

CHUNK = 64
N_HEADS = 8
HEAD_DIM = 64
N_KV_HEADS = 2
KV_GROUP = N_HEADS // N_KV_HEADS
ROPE_DIM = HEAD_DIM // 4
ROPE_THETA = 500000.0
N_IDX_HEADS = 8
IDX_DIM = 64
IDX_ROPE_DIM = IDX_DIM // 4
TOPK_MAX = 256
QUERY_BLOCK = 128
D_ATTN = N_HEADS * HEAD_DIM
D_CONV = 512
CONV_W = 31
MIX_WIDTH = D_ATTN + D_CONV
N_GROUPS = 4
EXPERTS_PER_GROUP = 4
N_EXPERTS = N_GROUPS * EXPERTS_PER_GROUP
TOP_K_EXPERTS = 2
D_EXPERT = 256
COLS_Q = D_ATTN
COLS_K = N_KV_HEADS * HEAD_DIM
COLS_V = N_KV_HEADS * HEAD_DIM
COLS_IQ = N_IDX_HEADS * IDX_DIM
COLS_IK = IDX_DIM
COLS_IW = N_IDX_HEADS
COLS_CONV = 2 * D_CONV
IN_COLS = COLS_Q + COLS_K + COLS_V + COLS_IQ + COLS_IK + COLS_IW + COLS_CONV
SPLIT_POINTS = (COLS_Q, COLS_Q + COLS_K, COLS_Q + COLS_K + COLS_V,
                COLS_Q + COLS_K + COLS_V + COLS_IQ,
                COLS_Q + COLS_K + COLS_V + COLS_IQ + COLS_IK,
                COLS_Q + COLS_K + COLS_V + COLS_IQ + COLS_IK + COLS_IW)
EPS = 1e-6

kernel_name = 'hymba_dsa_conformer_hmoe_stream_step'

def rms_norm(x, g):
    xf = x.astype(jnp.float32)
    y = xf * lax.rsqrt(jnp.mean(xf * xf, axis=-1, keepdims=True) + EPS)
    return (y * g.astype(jnp.float32)).astype(x.dtype)

def layer_norm(x, g, b):
    xf = x.astype(jnp.float32)
    mu = jnp.mean(xf, axis=-1, keepdims=True)
    xc = xf - mu
    var = jnp.mean(xc * xc, axis=-1, keepdims=True)
    y = xc * lax.rsqrt(var + EPS) * g.astype(jnp.float32) + b.astype(jnp.float32)
    return y.astype(x.dtype)

def partial_rope(x, pos, rot_dim):
    half = rot_dim // 2
    inv = ROPE_THETA ** (-jnp.arange(half, dtype=jnp.float32) / half)
    ang = pos.astype(jnp.float32)[:, None] * inv[None, :]
    cos = jnp.cos(ang)[:, None, :]
    sin = jnp.sin(ang)[:, None, :]
    xf = x.astype(jnp.float32)
    x1 = xf[..., :half]
    x2 = xf[..., half:rot_dim]
    out = jnp.concatenate([x1 * cos - x2 * sin, x2 * cos + x1 * sin, xf[..., rot_dim:]], axis=-1)
    return out.astype(x.dtype)

def dsa_query_block(blk, k_all, v_all, ik_all, k_chunk, k_top):
    q, qi, wi, q_chunk = blk
    B, QB = q.shape[0], q.shape[1]
    S = k_all.shape[1]
    dots = jnp.einsum('bqhd,bsd->bqhs', qi.astype(jnp.float32), ik_all)
    score = jnp.einsum('bqhs,bqh->bqs', jax.nn.relu(dots), wi.astype(jnp.float32))
    admissible = k_chunk[None, :] <= q_chunk[:, None]
    score = jnp.where(admissible[None], score, -jnp.inf)
    top_val, top_idx = lax.top_k(score, k_top)
    valid = jnp.isfinite(top_val)
    flat = top_idx.reshape(B, QB * k_top)
    bidx = jnp.arange(B)[:, None]
    k_sel = k_all.reshape(B, S, COLS_K)[bidx, flat].reshape(B, QB, k_top, N_KV_HEADS, HEAD_DIM)
    v_sel = v_all.reshape(B, S, COLS_V)[bidx, flat].reshape(B, QB, k_top, N_KV_HEADS, HEAD_DIM)
    qg = q.astype(jnp.float32).reshape(B, QB, N_KV_HEADS, KV_GROUP, HEAD_DIM)
    logits = jnp.einsum('bqngd,bqknd->bqngk', qg, k_sel) * (HEAD_DIM ** -0.5)
    logits = jnp.where(valid[:, :, None, None, :], logits, -jnp.inf)
    p = jax.nn.softmax(logits, axis=-1)
    o = jnp.einsum('bqngk,bqknd->bqngd', p, v_sel)
    return o.reshape(B, QB, D_ATTN).astype(q.dtype)

def dsa_attention(q, qi, wi, q_pos, k_all, v_all, ik_all, k_pos):
    B, T = q.shape[0], q.shape[1]
    S = k_all.shape[1]
    k_top = min(TOPK_MAX, S // 4)
    qb = QUERY_BLOCK if T % QUERY_BLOCK == 0 else T
    nb = T // qb

    def to_blocks(a):
        return jnp.moveaxis(a.reshape((B, nb, qb) + a.shape[2:]), 1, 0)

    k_f = k_all.astype(jnp.float32)
    v_f = v_all.astype(jnp.float32)
    ik_f = ik_all.astype(jnp.float32)
    k_chunk = k_pos // CHUNK
    q_chunk = (q_pos // CHUNK).reshape(nb, qb)
    out = lax.map(lambda blk: dsa_query_block(blk, k_f, v_f, ik_f, k_chunk, k_top),
                  (to_blocks(q), to_blocks(qi), to_blocks(wi), q_chunk))
    return jnp.moveaxis(out, 0, 1).reshape(B, T, D_ATTN)

def hybrid_mixer(h, pos, past, w_in, q_norm_g, k_norm_g, conv_w, conv_b, ln_conv_g, ln_conv_b):
    B, T = h.shape[0], h.shape[1]
    proj = h @ w_in
    q, k, v, iq, ik, iw, u = jnp.split(proj, SPLIT_POINTS, axis=-1)
    q = partial_rope(rms_norm(q.reshape(B, T, N_HEADS, HEAD_DIM), q_norm_g), pos, ROPE_DIM)
    k = partial_rope(rms_norm(k.reshape(B, T, N_KV_HEADS, HEAD_DIM), k_norm_g), pos, ROPE_DIM)
    v = v.reshape(B, T, N_KV_HEADS, HEAD_DIM)
    iq = partial_rope(iq.reshape(B, T, N_IDX_HEADS, IDX_DIM), pos, IDX_ROPE_DIM)
    ik = partial_rope(ik[:, :, None, :], pos, IDX_ROPE_DIM)[:, :, 0, :]
    iw = iw * (N_IDX_HEADS ** -0.5 * IDX_DIM ** -0.5)
    a, b = jnp.split(u, 2, axis=-1)
    g = a * jax.nn.sigmoid(b)
    if past is None:
        k_all, v_all, ik_all, k_pos = k, v, ik, pos
        conv_past = jnp.zeros((B, CONV_W - 1, D_CONV), g.dtype)
    else:
        k_past, v_past, ik_past, conv_past = past
        past_len = k_past.shape[1]
        k_all = jnp.concatenate([k_past.astype(k.dtype), k], axis=1)
        v_all = jnp.concatenate([v_past.astype(v.dtype), v], axis=1)
        ik_all = jnp.concatenate([ik_past.astype(ik.dtype), ik], axis=1)
        k_pos = jnp.concatenate([jnp.arange(past_len, dtype=jnp.int32), pos])
        conv_past = conv_past.astype(g.dtype)
    attn = dsa_attention(q, iq, iw, pos, k_all, v_all, ik_all, k_pos)
    padded = jnp.concatenate([conv_past, g], axis=1)
    y = lax.conv_general_dilated(padded, conv_w.astype(g.dtype)[:, None, :], window_strides=(1,),
                                 padding='VALID', dimension_numbers=('NWC', 'WIO', 'NWC'),
                                 feature_group_count=D_CONV) + conv_b
    y = jax.nn.silu(layer_norm(y, ln_conv_g, ln_conv_b))
    mix = jnp.concatenate([attn, y], axis=-1)
    return mix, (k, v, ik, padded[:, -(CONV_W - 1):])

def hierarchical_moe(h, w_router_group, b_router_group, w_router_expert, b_router_expert,
                     w_gate, w_up, w_down):
    B, T, D = h.shape
    hf = h.reshape(B * T, D)
    n = hf.shape[0]
    g_logits = (hf @ w_router_group + b_router_group).astype(jnp.float32)
    p_group = jax.nn.softmax(g_logits, axis=-1)
    g_sel = jnp.argmax(g_logits, axis=-1)
    p_g = jnp.take_along_axis(p_group, g_sel[:, None], axis=1)
    e_logits = (hf @ w_router_expert + b_router_expert).astype(jnp.float32)
    e_logits = e_logits.reshape(n, N_GROUPS, EXPERTS_PER_GROUP)
    e_in_group = jnp.take_along_axis(e_logits, g_sel[:, None, None], axis=1)[:, 0]
    p_e = jax.nn.softmax(e_in_group, axis=-1)
    top_p, top_i = lax.top_k(p_e, TOP_K_EXPERTS)
    top_p = top_p / jnp.sum(top_p, axis=-1, keepdims=True)
    weights = p_g * top_p
    expert_id = g_sel[:, None] * EXPERTS_PER_GROUP + top_i
    gate = jnp.sum(jax.nn.one_hot(expert_id, N_EXPERTS, dtype=jnp.float32) * weights[..., None], axis=1)
    hid = jax.nn.silu(jnp.einsum('nd,edf->nef', hf, w_gate)) * jnp.einsum('nd,edf->nef', hf, w_up)
    hid = hid * gate[:, :, None].astype(hid.dtype)
    out = jnp.einsum('nef,efd->nd', hid, w_down)
    return out.reshape(B, T, D)

def trunk_layer(x, c, pos, past, w_ada, b_ada, g_norm_mix, w_in, q_norm_g, k_norm_g, conv_w, conv_b,
                ln_conv_g, ln_conv_b, w_out, g_norm_ffn, w_router_group, b_router_group,
                w_router_expert, b_router_expert, w_gate, w_up, w_down):
    mod = (jax.nn.silu(c) @ w_ada + b_ada)[:, None, :]
    sh_a, sc_a, gt_a, sh_f, sc_f, gt_f = jnp.split(mod, 6, axis=-1)
    h = rms_norm(x, g_norm_mix) * (1 + sc_a) + sh_a
    mix, new_state = hybrid_mixer(h, pos, past, w_in, q_norm_g, k_norm_g, conv_w, conv_b,
                                  ln_conv_g, ln_conv_b)
    x = x + gt_a * (mix @ w_out)
    h = rms_norm(x, g_norm_ffn) * (1 + sc_f) + sh_f
    x = x + gt_f * hierarchical_moe(h, w_router_group, b_router_group, w_router_expert,
                                    b_router_expert, w_gate, w_up, w_down)
    return x, new_state

def setup_inputs(seed: int = 0) -> dict:
    key = jax.random.key(seed)
    ks = jax.random.split(key, 32)
    f32 = jnp.float32

    def nrm(k, shape, scale):
        return jax.random.normal(k, shape, f32) * scale

    return {
        'x_prompt': nrm(ks[0], (BATCH, SEQ, D_MODEL), 1.0),
        'x_sample': nrm(ks[1], (DEC_BATCH, DEC_SEQ, D_MODEL), 1.0),
        'c_prompt': nrm(ks[2], (BATCH, D_MODEL), 1.0),
        'c_sample': nrm(ks[3], (DEC_BATCH, D_MODEL), 1.0),
        'cache_k': nrm(ks[4], (DEPTH, DEC_BATCH, PAST_LEN, N_KV_HEADS, HEAD_DIM), 1.0),
        'cache_v': nrm(ks[5], (DEPTH, DEC_BATCH, PAST_LEN, N_KV_HEADS, HEAD_DIM), 1.0),
        'cache_idx_k': nrm(ks[6], (DEPTH, DEC_BATCH, PAST_LEN, IDX_DIM), 1.0),
        'state_conv': nrm(ks[7], (DEPTH, DEC_BATCH, CONV_W - 1, D_CONV), 0.5),
        'w_ada': nrm(ks[8], (DEPTH, D_MODEL, 6 * D_MODEL), 0.5 * D_MODEL ** -0.5),
        'b_ada': nrm(ks[9], (DEPTH, 6 * D_MODEL), 0.01),
        'g_norm_mix': 1.0 + nrm(ks[10], (DEPTH, D_MODEL), 0.01),
        'w_in': nrm(ks[11], (DEPTH, D_MODEL, IN_COLS), D_MODEL ** -0.5),
        'q_norm_g': 1.0 + nrm(ks[12], (DEPTH, HEAD_DIM), 0.01),
        'k_norm_g': 1.0 + nrm(ks[13], (DEPTH, HEAD_DIM), 0.01),
        'conv_w': nrm(ks[14], (DEPTH, CONV_W, D_CONV), CONV_W ** -0.5),
        'conv_b': nrm(ks[15], (DEPTH, D_CONV), 0.01),
        'ln_conv_g': 1.0 + nrm(ks[16], (DEPTH, D_CONV), 0.01),
        'ln_conv_b': nrm(ks[17], (DEPTH, D_CONV), 0.01),
        'w_out': nrm(ks[18], (DEPTH, MIX_WIDTH, D_MODEL), MIX_WIDTH ** -0.5),
        'g_norm_ffn': 1.0 + nrm(ks[19], (DEPTH, D_MODEL), 0.01),
        'w_router_group': nrm(ks[20], (DEPTH, D_MODEL, N_GROUPS), D_MODEL ** -0.5),
        'b_router_group': nrm(ks[21], (DEPTH, N_GROUPS), 0.01),
        'w_router_expert': nrm(ks[22], (DEPTH, D_MODEL, N_EXPERTS), D_MODEL ** -0.5),
        'b_router_expert': nrm(ks[23], (DEPTH, N_EXPERTS), 0.01),
        'w_gate': nrm(ks[24], (DEPTH, N_EXPERTS, D_MODEL, D_EXPERT), D_MODEL ** -0.5),
        'w_up': nrm(ks[25], (DEPTH, N_EXPERTS, D_MODEL, D_EXPERT), D_MODEL ** -0.5),
        'w_down': nrm(ks[26], (DEPTH, N_EXPERTS, D_EXPERT, D_MODEL), D_EXPERT ** -0.5),
    }

def reference(x_prompt, x_sample, c_prompt, c_sample, cache_k, cache_v, cache_idx_k, state_conv,
              w_ada, b_ada, g_norm_mix, w_in, q_norm_g, k_norm_g, conv_w, conv_b, ln_conv_g,
              ln_conv_b, w_out, g_norm_ffn, w_router_group, b_router_group, w_router_expert,
              b_router_expert, w_gate, w_up, w_down):
    def params_at(l):
        return (w_ada[l], b_ada[l], g_norm_mix[l], w_in[l], q_norm_g[l], k_norm_g[l], conv_w[l],
                conv_b[l], ln_conv_g[l], ln_conv_b[l], w_out[l], g_norm_ffn[l], w_router_group[l],
                b_router_group[l], w_router_expert[l], b_router_expert[l], w_gate[l], w_up[l],
                w_down[l])

    x = x_prompt
    pos_p = jnp.arange(x_prompt.shape[1], dtype=jnp.int32)
    st_p = []
    for l in range(DEPTH):
        x, st = trunk_layer(x, c_prompt, pos_p, None, *params_at(l))
        st_p.append(st)
    y_prompt = x

    past_len = cache_k.shape[2]
    x = x_sample
    pos_s = past_len + jnp.arange(x_sample.shape[1], dtype=jnp.int32)
    st_s = []
    for l in range(DEPTH):
        x, st = trunk_layer(x, c_sample, pos_s, (cache_k[l], cache_v[l], cache_idx_k[l], state_conv[l]),
                            *params_at(l))
        st_s.append(st)
    y_sample = x

    new_k_prompt = jnp.stack([s[0] for s in st_p])
    new_v_prompt = jnp.stack([s[1] for s in st_p])
    new_idx_k_prompt = jnp.stack([s[2] for s in st_p])
    new_conv_prompt = jnp.stack([s[3] for s in st_p])
    new_k_sample = jnp.stack([s[0] for s in st_s])
    new_v_sample = jnp.stack([s[1] for s in st_s])
    new_idx_k_sample = jnp.stack([s[2] for s in st_s])
    new_conv_sample = jnp.stack([s[3] for s in st_s])
    return (y_prompt, y_sample, new_k_prompt, new_v_prompt, new_idx_k_prompt, new_conv_prompt,
            new_k_sample, new_v_sample, new_idx_k_sample, new_conv_sample)


_drawn_inputs = setup_inputs


def setup_inputs(seed=0):
    import zlib

    import numpy as np

    out = dict(_drawn_inputs(seed))
    spreads = {}
    factors = {'b_ada': 3.273,
     'g_norm_mix': 5.235,
     'q_norm_g': 8.0,
     'k_norm_g': 5.496,
     'conv_b': 8.0,
     'ln_conv_g': 8.0,
     'ln_conv_b': 8.0,
     'g_norm_ffn': 7.274,
     'b_router_group': 21.427,
     'b_router_expert': 5.273}
    for name, (base, spread) in spreads.items():
        noise = np.random.default_rng([zlib.crc32(name.encode()), seed]).standard_normal(out[name].shape)
        drawn = base * np.exp(spread * noise) if base else spread * noise
        out[name] = __import__('jax').numpy.asarray(drawn.astype(out[name].dtype))
    for name, factor in factors.items():
        out[name] = (out[name] * factor).astype(out[name].dtype)
    return out
```

```python
from contextlib import ExitStack

import numpy as np
import concourse.bass as bass
from concourse import mybir

F32 = mybir.dt.float32
F16 = mybir.dt.float16
I32 = mybir.dt.int32
U32 = mybir.dt.uint32
ALU = mybir.AluOpType
ACT = mybir.ActivationFunctionType
AX = mybir.AxisListType

P = 128
DEPTH = 2
D = 1024
KC = D // P
SEQ, DEC, PAST = 512, 64, 512
NT = 5
TOK = SEQ + DEC
HD = 64
ROT = 8
CW = 31
NE = 16
DE = 256
EPS = 1e-6
BIG = 1e30
MARK = -3e38
XJ = (2 * TOK - 1) // P
XROW = NE * P
IW_SCALE = float(np.float32(8 ** -0.5 * 64 ** -0.5))
CQ, CK, CV, CIQ, CIK, CIW, CU = 0, 512, 640, 768, 1280, 1344, 1352
K_ID, K_UT, K_ONE, K_IOTA, K_M0 = 0, 128, 256, 384, 512
K_COS, K_SIN, K_TOK, K_E16, K_ROW, NCONST = 640, 680, 720, 725, 741, 757


def constants():
    c = np.zeros((P, NCONST), np.float32)
    i = np.arange(P)
    c[:, K_ID:K_ID + P] = np.eye(P)
    c[:, K_UT:K_UT + P] = i[:, None] < i[None, :]
    c[:, K_ONE:K_ONE + P] = 1.0
    c[:, K_IOTA:K_IOTA + P] = i[None, :]
    c[:64, K_M0 + 64:K_M0 + P] = -BIG
    inv = np.float32(500000.0) ** (-np.arange(ROT, dtype=np.float32) / np.float32(ROT))
    pos = (np.arange(NT)[None, :] * P + i[:, None]).astype(np.float32)
    ang = pos[:, :, None] * inv[None, None, :].astype(np.float32)
    c[:, K_COS:K_COS + 40] = np.cos(ang).reshape(P, 40)
    c[:, K_SIN:K_SIN + 40] = np.sin(ang).reshape(P, 40)
    c[:, K_TOK:K_TOK + NT] = pos
    c[:, K_E16:K_E16 + NE] = np.arange(NE)[None, :]
    c[:, K_ROW:K_ROW + NE] = np.arange(NE)[None, :] * P
    return c


def rows_of(t):
    return P if t < 4 else DEC


PARTS = ((P, 0, 4), (DEC, 4, 5))
SCORED = (4, 3, 2, 1)
NKEYS = {0: 128, 1: 256, 2: 384, 3: 512, 4: 576}
TOPK = {1: 128, 2: 128, 3: 128, 4: 144}
MSK_AT = {1: 0, 2: 256, 3: 640, 4: 1152}
ATTN = (0, 4, 3, 2, 1)
NSMALL = 18
DVE_CONV = 3
NCDVE, NCPOOL = DVE_CONV * CW, (4 - DVE_CONV) * CW
S_SS, S_VAR, S_RS, S_M8, S_QS, S_MX, S_NMX, S_SUM, S_INV = 0, 5, 10, 16, 24, 124, 132, 140, 156
S_FS, S_FV, S_FR, S_AT = 164, 169, 174, 180
R_LG, R_GM, R_EQ, R_CAND, R_MI, R_GOH, R_GE, R_EM, R_M1 = 0, 100, 105, 125, 145, 150, 170, 190, 270
R_EQ1, R_MI1, R_OH1, R_M2, R_OH2, R_Z, R_W, R_G1, R_G2 = 275, 355, 360, 440, 445, 525, 530, 550, 555
R_PG, R_AS, R_POS, R_TMP, R_S = 560, 565, 645, 725, 805


def program(nc, A, O):
    ctx = ExitStack()
    with ctx:
        def sb(name, shape, dt=F32):
            return ctx.enter_context(nc.sbuf_tensor(name, shape, dt))

        def sem(name):
            return ctx.enter_context(nc.semaphore(name))

        def dram(name, shape):
            return nc.dram_tensor(name, shape, F32, kind="Internal").ap()

        W = sb("W", [P, 6, 2048])
        C = sb("C", [P, NCONST])
        X = sb("X", [P, NT, D])
        hT = sb("hT", [P, KC, TOK])
        gt = sb("gt", [P, 2, D])
        vrows = sb("vrows", [52, P])
        vT = sb("vT", [P, 52])
        crows = sb("crows", [62, 512])
        taps = sb("taps", [P, 4, CW])
        gq = sb("gq", [P, 2, HD])
        wr = sb("wr", [P, KC, 20])
        rb = sb("rb", [P, 20])
        ck = sb("ck", [P, 4, P])
        cv = sb("cv", [P, 4, P])
        cik = sb("cik", [P, 4, P])
        vrow = sb("vrow", [P, NT, P])
        iw = sb("iw", [P, NT, 8])
        small = sb("small", [P, 200])
        jobs = sb("jobs", [P, XJ + 1], I32)
        idx = sb("idx", [P, NE + 1], U32)
        zeros = sb("zeros", [P, 256])
        sid = sb("sid", [P, 2 * NT], U32)
        route = sb("route", [P, 816])
        tokf = sb("tokf", [P, NT], F16)
        ctmp = sb("ctmp", [P, 2, 606])
        arena = sb("arena", [P, 22320])

        def part(at, n, *shape):
            v = arena[:, at:at + n]
            if len(shape) == 2:
                return v.rearrange("p (a b) -> p a b", a=shape[0])
            if len(shape) == 3:
                return v.rearrange("p (a b c) -> p a b c", a=shape[0], b=shape[1])
            return v

        iqr = part(0, 3200, NT, 10, HD)
        qkr = part(3200, 3200, NT, 10, HD)
        iqf, qkf = part(0, 3200, NT, 640), part(3200, 3200, NT, 640)
        qT = part(6400, 2304, 4, TOK)
        kT = [part(8704, 1088), part(9792, 1088)]
        gT = part(10880, 2544, 4, 636)
        cy = part(0, 2424, 4, 606)
        orow = part(2424, 512)
        msk = part(13424, 1728)
        XN = part(15152, 5120, NT, D)
        rel = part(15152, 1728, 3, 576)
        sq = part(15152, 3200, NT, 10, HD)
        PR = part(15152, 4608, 8, 576)
        pT = part(19760, 2560, 5, 512)
        glu = part(19760, 2304, 4, 576)
        lnb = part(15152, 576)
        sqc = part(16880, 2304, 4, 576)
        wtmp = part(13424, 1024, 2, 512)
        AB = part(0, 4096, 2, 2, D)
        gf = part(4096, 1024)
        HR = part(5120, 2048, 2, D)
        oh = part(7168, 2048).bitcast(F16).rearrange("p (a e s) -> p a e s", a=2, e=NE)
        ohx = part(7168, 640).bitcast(F16).rearrange("p (a s) -> p a s", a=2 * NT)
        xg = part(9216, 2048, 2, D)
        xgT = part(11264, 2048, 2 * KC, P)
        sg = part(13312, 512, 2, DE)
        hid = part(13824, 512, 2, DE)
        hidT = part(14336, 512, 4, P)
        ys = part(14848, 2048, 2, D)
        yg = part(16896, 4096, 4, D)
        junk = part(20272, 1024)
        srows = part(0, 128)
        brows = part(128, 128)
        scT = part(256, 16, 2, KC)
        baT = part(272, 96)
        modT = part(368, 192, 4, 48)
        modf = part(368, 192)
        mrow = part(560, 256, 2, P)

        ps = [ctx.enter_context(nc.psum_tensor(f"ps{i}", [P, 512], F32)) for i in range(8)]

        mod_d = dram("mod_d", [DEPTH, 2, 6, D])
        h_d = dram("h_d", [TOK, D])
        y_d = dram("y_d", [XROW + XJ * P, D])

        ident = C[:, K_ID:K_ID + P]
        ones = C[:, K_ONE:K_ONE + P]

        w_ld = [sem(f"w_ld{i}") for i in range(6)]
        w_free = [sem(f"w_free{i}") for i in range(6)]
        s_c, s_x, s_r = sem("s_c"), sem("s_x"), sem("s_r")
        s_silu, s_cT, s_cTc, s_ada, s_adae = (sem(n) for n in ("s_silu", "s_cT", "s_cTc", "s_ada", "s_adae"))
        s_mT, s_mTc, s_mst = sem("s_mT"), sem("s_mTc"), sem("s_mst")
        s_init = sem("s_init")
        s_xg = [sem(f"s_xg{i}") for i in range(2)]
        s_yg = [sem(f"s_yg{i}") for i in range(2)]
        s_xx = sem("s_xx")
        n_cnt = sem("n_cnt")
        y_out = sem("y_out")
        s_fin = sem("s_fin")
        sp_steps = sem("sp_steps")
        go = {n: sem(f"go_{n}") for n in ("pe", "act", "pool")}
        arrived = sem("arrived")
        names = ("small_ld", "gt_ld", "gtf_ld", "ab_ld", "vecT", "vecC", "sumsq", "var", "root", "xn", "nT", "nTa", "nTd",
                 "proj", "proja", "ropei", "dch", "pch", "tr", "tra", "dots", "rel", "score", "sqd", "qvar", "qroot",
                 "qinv", "ropeq", "uproj", "glua", "glup", "cdve", "cpool", "mask", "lgt", "ttr", "nmx", "pexp", "pt",
                 "pta", "pv", "on", "oT", "lnm", "lnx", "lnsq", "lnv", "lnr", "lny", "mixy", "wo", "wod", "xadd",
                 "fsum", "fvar", "froot", "hrow", "hst0", "hst1", "hTt", "hTa", "rl", "gdiff", "gexp", "zdiff", "zexp",
                 "assign", "pos", "ready", "cst", "csta", "outst", "comb", "zst",
                 "oh", "ohu", "idx", "tx", "txa", "txd", "gu", "sg", "hid", "ht", "hta", "dn", "ya", "yd", "yst0", "yst1")
        L = {n: sem("l_" + n) for n in names}
        names = ("oh", "idx", "idc", "tx", "txa", "txd", "gu", "sg", "hid", "ht", "hta", "dn", "ya", "yd", "yst", "rch")
        M = {n: sem("x_" + n) for n in names}
        lrange = range(min(s.num for s in L.values()), max(s.num for s in L.values()) + 1)
        mrange = range(min(s.num for s in M.values()), max(s.num for s in M.values()) + 1)
        assert len(lrange) == len(L) and len(mrange) == len(M)

        block = ctx.enter_context(nc.Block())

        def leave(eng, name):
            eng.drain().then_inc(arrived, 1)
            eng.wait_ge(go[name], 1)
            eng.sem_clear(go[name])

        def release(dve, sems):
            dve.drain()
            dve.wait_ge(arrived, 3)
            dve.sem_clear(arrived)
            dve.sem_clear(sems)
            for g in go.values():
                dve.sem_inc(g, 1)

        def keys_of(t):
            return (0, NKEYS[t]) if t < 4 else (512, 1024)

        def chunks_of(t):
            return [(c, P) for c in range(t + 1 if t < 4 else 4)] + ([(4, DEC)] if t == 4 else [])

        GROUPS = [(t, g) for t in ATTN for g in range(2)]
        PT0 = [sum(len(chunks_of(t)) for t, _ in GROUPS[:n]) for n in range(11)]
        TJ = [PT0[n] + max(0, (n - 1) // 2) for n in range(11)]

        def logit_bank(job):
            return job % 3 if job < 8 else job % 2 if job < 16 else (job + 2) % 3

        def rope(eng, E, rows, r, t0, t1, at, s_chain, n_chain, done):
            nt = t1 - t0
            shape = [r, nt, 10, ROT]

            def angle(k):
                return C[0:r, k + ROT * t0:k + ROT * t1].rearrange("p (t d) -> p t d", d=ROT).unsqueeze(2).to_broadcast(shape)
            x1, x2 = rows[0:r, t0:t1, :, 0:ROT], rows[0:r, t0:t1, :, ROT:2 * ROT]
            tmp = [arena[0:r, at + 400 * j:at + 400 * j + nt * 10 * ROT].rearrange("p (t h d) -> p t h d", t=nt, h=10) for j in range(4)]
            for j, (x, k) in enumerate(((x1, K_COS), (x2, K_SIN), (x2, K_COS), (x1, K_SIN))):
                n_chain[0] += 1
                E.tensor_tensor(tmp[j], x, angle(k), ALU.mult).then_inc(s_chain, 1)
            eng.wait_ge(s_chain, n_chain[0])
            n_chain[0] += 1
            E.tensor_tensor(x1, tmp[0], tmp[1], ALU.subtract).then_inc(s_chain, 1)
            E.tensor_tensor(x2, tmp[2], tmp[3], ALU.add).then_inc(done, 1)
            eng.wait_ge(s_chain, n_chain[0])
            eng.wait_ge(done, 1 if t0 == 0 else 2)

        @block.sync
        def _(sp):
            n0 = sp.alloc_register("sp_uses_012")
            n3 = sp.alloc_register("sp_uses_3")
            n4 = sp.alloc_register("sp_uses_45")
            further = sp.alloc_register("sp_further")
            expert = sp.alloc_register("sp_expert")

            def wait(s, value):
                sp.wait_ge(s, value)
                sp.sem_inc(sp_steps, 1)

            def load(slot, use, src):
                if not (isinstance(use, int) and use == 0):
                    wait(w_free[slot], use)
                n = src.shape[-1] * src.shape[-2]
                dst = W[:, slot, :]
                dst = dst[:, 0:n].rearrange("p (k c) -> p k c", c=src.shape[-1])
                sp.dma_start(dst, src).then_inc(w_ld[slot], 16)

            wada = A["w_ada"].rearrange("l (k p) c -> l p k c", p=P)
            win = A["w_in"].rearrange("l (k p) c -> l p k c", p=P)
            wout = A["w_out"].rearrange("l (k p) c -> l p k c", p=P)
            wexp = [A[n].rearrange("l e (k p) f -> l e p k f", p=P) for n in ("w_gate", "w_up", "w_down")]

            def ada(l, third, first=False):
                for c in range(3):
                    for hf in range(2):
                        src = wada[l, :, 4 * hf:4 * hf + 4, bass.ds(third * 1536 + c * 512, 512)]
                        load(2 * c + hf, 0 if first else third + 4 * l, src)

            ada(0, 0, True)
            with sp.Fori(1, 4) as third:
                ada(0, third)
            with sp.Fori(0, 4) as third:
                ada(1, third)
            sp.reg_mov(n0, 8)
            sp.reg_mov(n3, 8)
            sp.reg_mov(n4, 8)

            with sp.Fori(0, DEPTH) as l:
                b0, b3, b4 = sp.snap(n0), sp.snap(n3), sp.snap(n4)
                base = [b0, b0, b0, b3, b4, b4]
                for c in range(8):
                    for hf in range(2):
                        s = 2 * (c % 3) + hf
                        ks = slice(4 * hf, 4 * hf + 4)

                        def cols(w, c0, c1):
                            return w[bass.ds(l, 1), :, ks, c0:c1].rearrange("l p k c -> (l p) k c")
                        if c in (4, 5):
                            c0 = CU + 512 * hf + 256 * (c - 4)
                            src = win[bass.ds(l, 1), :, :, c0:c0 + 256].rearrange("l p k c -> (l p) k c")
                        else:
                            src = {0: lambda: cols(win, CIQ, CIK), 1: lambda: cols(win, CIK, CU), 2: lambda: cols(win, CK, CIQ),
                                   3: lambda: cols(win, CQ, CK), 6: lambda: cols(wout, 0, 512),
                                   7: lambda: cols(wout, 512, 1024)}[c]()
                        load(s, base[s] + c // 3, src)
                with sp.Fori(0, NE // 2) as i:
                    for u in range(2):
                        for j, w in enumerate(wexp):
                            s = 3 * u + j
                            src = w[bass.ds(l, 1), bass.ds(i * 2 + u, 1)].rearrange("l e p k f -> (l e p) k f")
                            load(s, base[s] + (3 if s < 4 else 2) + i, src)
                sp.reg_add(n0, n0, 11)
                sp.reg_add(n3, n3, 11)
                sp.reg_add(n4, n4, 10)
                wait(n_cnt, l + 1)
                sp.reg_load(further, jobs[0:1, XJ:XJ + 1])
                with sp.If_ne(further, 0):
                    with sp.Fori(0, sp.snap(further, min_val=0, max_val=XJ)) as x:
                        sp.reg_load(expert, jobs[0:1, bass.ds(x, 1)])
                        e = sp.snap(expert, min_val=0, max_val=NE - 1)
                        for s, w in enumerate(wexp):
                            load(s, sp.snap(n0), w[bass.ds(l, 1), bass.ds(e, 1)].rearrange("l e p k f -> (l e p) k f"))
                        sp.reg_add(n0, n0, 1)
            sp.wait_ge(s_x, 32)

        @block.tensor
        def _(pe):
            T = nc.tensor
            n0 = pe.alloc_register("pe_uses_012")
            n3 = pe.alloc_register("pe_uses_3")
            n4 = pe.alloc_register("pe_uses_45")
            further = pe.alloc_register("pe_further")
            gathers = pe.alloc_register("pe_gathers")
            pe.reg_mov(gathers, 0)
            done_units = []

            def count(ins, done):
                if done is not None:
                    ins.then_inc(done, 1)
                elif done_units:
                    ins.then_inc(w_free[done_units.pop(0)], 1)

            def products(out, pairs, done=None, before=None, halfway=None):
                for n, (l, r) in enumerate(pairs):
                    if before is not None and n == len(pairs) // 2:
                        before()
                    ins = T.matmul(out, l, r, start=n == 0, stop=n == len(pairs) - 1, skip_group_check=True)
                    if halfway is not None and n == len(pairs) // 2:
                        assert not done_units
                        done_units.append(halfway)
                    count(ins, done if n == len(pairs) - 1 else None)

            def turn(outs_ins, done):
                for n, (o, i) in enumerate(outs_ins):
                    m = i.shape[0]
                    count(T.transpose(o, i, ident[0:m, 0:m]), done if n == len(outs_ins) - 1 else None)

            pe.wait_ge(s_c, 16)
            pe.wait_ge(s_r, 32)
            pe.wait_ge(s_silu, 1)
            turn([(ps[7][:, 0:16], srows[0:16, :]), (ps[7][:, 128:224], brows[0:96, :])], s_cT)
            pe.wait_ge(s_cTc, 2)
            with pe.Fori(0, DEPTH) as l:
                with pe.Fori(0, 2) as h:
                    for u in range(2):
                        g = l * 4 + h * 2 + u
                        for c in range(3):
                            pe.wait_ge(w_ld[2 * c], (g + 1) * 16)
                            pe.wait_ge(w_ld[2 * c + 1], (g + 1) * 16)
                            if c == 0:
                                pe.wait_ge(s_adae, g + 1)
                            for d in range(4):
                                j = (4 * c + d) * 2
                                for k in range(KC):
                                    w = W[:, 2 * c + k // 4, :].rearrange("p (k c) -> p k c", c=512)
                                    ins = T.matmul(ps[u][:, j:j + 2], w[:, k % 4, d * P:(d + 1) * P], scT[:, :, k],
                                                   start=k == 0, stop=k == KC - 1, skip_group_check=True)
                                    if c == 2 and d == 3 and k == KC - 1:
                                        count(ins, s_ada)
                                    else:
                                        count(ins, None)
                            if c < 2:
                                done_units += [2 * c, 2 * c + 1]
                        for q in range(2):
                            T.transpose(ps[6][:, 0:128], ident, ident).then_inc(w_free[4 + q], 1)
            for l in range(DEPTH):
                pe.wait_ge(s_adae, 10)
                turn([(ps[2 + l][0:96, 0:P], modf[:, 96 * l:96 * l + 96])], s_mT)
            pe.reg_mov(n0, 8)
            pe.reg_mov(n3, 8)
            pe.reg_mov(n4, 8)
            with pe.Fori(0, DEPTH) as l:
                b0, b3, b4 = pe.snap(n0), pe.snap(n3), pe.snap(n4)
                base = [b0, b0, b0, b3, b4, b4]

                def came(s, use):
                    pe.wait_ge(w_ld[s], (base[s] + use + 1) * 16)

                pe.wait_ge(L["small_ld"], 16 * NSMALL)
                turn([(ps[6][:, 0:52], vrows[0:52, :])], L["vecT"])
                turn([(ps[7][:, 61 * c:61 * c + 61], crows[0:61, c * P:(c + 1) * P]) for c in range(4)], L["vecT"])
                pe.wait_ge(L["xn"], NT)
                for k in range(KC):
                    if k == 6:
                        pe.wait_ge(L["vecC"], 4)
                    turn([(ps[k][:, t * P:(t + 1) * P], XN[:, t, k * P:(k + 1) * P]) for t in range(4)], L["nT"])
                for q, s_read in ((0, "nTa"), (1, "nTd")):
                    pe.wait_ge(L[s_read], 1)
                    turn([(ps[q][:, k * DEC:(k + 1) * DEC], XN[0:DEC, 4, k * P:(k + 1) * P]) for k in range(q, KC, 2)], L["nT"])
                pe.wait_ge(L["nTa"], 8)
                pe.wait_ge(L["nTd"], 8)

                def tokens(t):
                    return slice(t * P, t * P + rows_of(t))

                def project(c, n, job, ring, evac, done, lag):
                    s = 2 * (c % 3)
                    wv = [W[:, s + q, 0:4 * n].rearrange("p (k c) -> p k c", c=n) for q in range(2)]
                    for t in range(NT):
                        if job + t >= len(ring) or lag:
                            pe.wait_ge(evac, job + t - len(ring) + 1)
                        if t == 0:
                            came(s, c // 3)
                        products(ps[ring[(job + t) % len(ring)]][0:rows_of(t), 0:n],
                                 [(hT[:, k, tokens(t)], wv[k // 4][:, k % 4, :]) for k in range(KC)], done,
                                 before=(lambda: came(s + 1, c // 3)) if t == 0 else None,
                                 halfway=s if t == NT - 1 else None)
                    done_units.append(s + 1)

                for n, (c, w) in enumerate(((0, 512), (1, 72), (2, 256))):
                    project(c, w, 5 * n, (0, 1, 2), L["proja"], L["proj"], False)

                def turn_qk(src, past, job):
                    for i in range(5):
                        turn([(ps[3 + i][:, t * P:(t + 1) * P], src[:, t, i * P:(i + 1) * P]) for t in range(4)], L["tr"])
                    pe.wait_ge(L["tra"], job + 1)
                    turn([(ps[3][:, i * DEC:(i + 1) * DEC], src[0:DEC, 4, i * P:(i + 1) * P]) for i in range(5)], L["tr"])
                    pe.wait_ge(L["tra"], job + 2)
                    turn([(ps[4][:, c * P:(c + 1) * P], past[:, c]) for c in range(4)], L["tr"])
                pe.wait_ge(L["ropei"], 2)
                turn_qk(iqf, cik, 0)
                pe.wait_ge(L["tra"], 7)
                for n, (t, h) in enumerate((t, h) for t in SCORED for h in range(8)):
                    if n >= 3:
                        pe.wait_ge(L["rel"], n - 2)
                    hp = slice(64 * (h % 2), 64 * (h % 2) + 64)
                    a, b = keys_of(t)
                    q = qT[hp, h // 2, tokens(t)]
                    if t == 4:
                        if n >= 2:
                            pe.wait_ge(L["rel"], n - 1)
                        count(T.matmul(ps[3 + n % 2][0:DEC, 0:DEC], q, kT[0][hp, 1024:1088], start=True, stop=True), None)
                    count(T.matmul(ps[5 + n % 3][0:rows_of(t), 0:b - a], q, kT[0][hp, a:b], start=True, stop=True), L["dots"])
                project(3, 512, 15, (0, 1, 2), L["proja"], L["proj"], False)
                pe.wait_ge(L["rel"], 32)
                for i in range(4):
                    if i == 1:
                        pe.wait_ge(L["proja"], 20)
                    c = 4 + i // 2
                    s = 2 * (c % 3)
                    if i >= 2:
                        pe.wait_ge(L["glua"], i - 1)
                    for n, (ab, smp) in enumerate(((0, 0), (1, 0), (0, 1), (1, 1))):
                        out = ps[7 if i % 2 == 0 else 2][:, ab * DEC:(ab + 1) * DEC] if smp else ps[3 + 2 * (i % 2) + ab][:, 0:SEQ]
                        tk = slice(SEQ, TOK) if smp else slice(0, SEQ)
                        if i % 2 == 0 and not smp:
                            came(s + ab, c // 3)
                        wv = W[:, s + ab, :].rearrange("p (k c) -> p k c", c=256)
                        products(out, [(wv[:, k, (i % 2) * P:(i % 2) * P + P], hT[:, k, tk]) for k in range(KC)], L["uproj"])
                        if i % 2 == 1 and smp:
                            done_units.append(s + ab)
                pe.wait_ge(L["ropeq"], 2)
                pe.wait_ge(L["glua"], 4)
                turn_qk(qkf, ck, 7)
                pe.wait_ge(L["tra"], 14)
                pe.wait_ge(L["glup"], 4)
                turn([(ps[6][0:30, c * P:(c + 1) * P], gT[:, c, 512:542]) for c in range(4)], L["cst"])
                turn([(ps[7][0:30, c * P:(c + 1) * P], gT[:, c, 606:636]) for c in range(4)], L["cst"])

                def logits(n):
                    t, g = GROUPS[n]
                    a, b = keys_of(t)
                    hp = slice(64 * g, 64 * g + 64)
                    for i in range(4):
                        job = 4 * n + i
                        if job >= 3:
                            pe.wait_ge(L["ttr"], job - 1 if 2 <= n <= 4 else job - 2)
                        q = qT[hp, i, tokens(t)]
                        if t == 4:
                            T.matmul(ps[2 + job % 2][0:DEC, 0:DEC], q, kT[1][hp, 1024:1088], start=True, stop=True)
                        T.matmul(ps[logit_bank(job)][0:rows_of(t), 0:b - a], q, kT[1][hp, a:b], start=True, stop=True).then_inc(L["lgt"], 1)

                tj = [0]

                def bank_for_turn():
                    j = tj[0]
                    if j >= 2:
                        pe.wait_ge(L["pta"], j - 1)
                    tj[0] += 1
                    return ps[4 + j % 2]

                def turn_output(n):
                    m = rows_of(GROUPS[n][0])
                    o = bank_for_turn()
                    pe.wait_ge(L["on"], n // 2 + 1)
                    turn([(o[:, j * m:(j + 1) * m], orow[0:m, j * P:(j + 1) * P]) for j in range(4)], L["pt"])

                logits(0)
                logits(1)
                pe.wait_ge(L["csta"], 2)
                for n, (t, g) in enumerate(GROUPS):
                    m = rows_of(t)
                    pe.wait_ge(L["pexp"], n + 1)
                    assert tj[0] == TJ[n]
                    for c, kn in chunks_of(t):
                        o = bank_for_turn()
                        turn([(o[0:kn, i * m:(i + 1) * m], PR[0:m, 4 * (n % 2) + i, c * P:c * P + kn]) for i in range(4)], L["pt"])
                    if n + 2 < len(GROUPS):
                        logits(n + 2)
                    if n >= 2 and n % 2 == 0:
                        turn_output(n - 1)
                    if g == 0 and n >= 4:
                        pe.wait_ge(L["on"], n // 2 - 1)
                    last = chunks_of(t)[-1][0]
                    pe.wait_ge(L["pta"], TJ[n] + len(chunks_of(t)))
                    for i in range(4):
                        h = 4 * g + i
                        for c, kn in chunks_of(t):
                            v = (vrow[0:kn, c, :] if t < 4 else cv[:, c, :] if c < 4 else vrow[0:kn, 4, :])[:, g * 64:g * 64 + 64]
                            ins = T.matmul(ps[6 + (n // 2) % 2][0:m, h * 64:(h + 1) * 64], pT[0:kn, c, i * m:(i + 1) * m], v,
                                           start=c == 0, stop=c == last, skip_group_check=True)
                    ins.then_inc(L["pv"], 1)
                turn_output(9)
                pe.wait_ge(L["ttr"], 40)
                pe.wait_ge(L["cdve"], NCDVE)
                pe.wait_ge(L["cpool"], NCPOOL)
                products(ps[0][:, 0:SEQ], [(ones, cy[:, c, 0:SEQ]) for c in range(4)], L["lnm"])
                products(ps[1][:, 0:DEC], [(ones, cy[:, c, 542:606]) for c in range(4)], L["lnm"])
                pe.wait_ge(L["lnsq"], 2)
                products(ps[2][:, 0:SEQ], [(ones, sqc[:, c, 0:SEQ]) for c in range(4)], L["lnv"])
                products(ps[3][:, 0:DEC], [(ones, sqc[:, c, SEQ:TOK]) for c in range(4)], L["lnv"])
                pe.wait_ge(L["mixy"], 8)
                pe.wait_ge(L["pta"], TJ[10] + 1)
                for n, c in enumerate((6, 7)):
                    project(c, 512, 5 * n, (4, 5, 6, 7), L["wod"], L["wo"], False)
                for t in range(NT):
                    m = rows_of(t)
                    pe.wait_ge(L["hrow"], t + 1)
                    if t >= 2:
                        pe.wait_ge(L["hTa"], 2 * (t - 1))
                    for q in range(2):
                        turn([(ps[2 * (t % 2) + q][:, j * m:(j + 1) * m], HR[0:m, t % 2, (4 * q + j) * P:(4 * q + j + 1) * P])
                              for j in range(4)], L["hTt"])
                pe.wait_ge(L["wod"], 10)
                for t in range(NT):
                    pe.wait_ge(L["hTa"], 2 * (t + 1))
                    products(ps[4][0:rows_of(t), t * 20:t * 20 + 20], [(hT[:, k, tokens(t)], wr[:, k, :]) for k in range(KC)], L["rl"])
                assert not done_units
                pe.wait_ge(L["assign"], 1)
                sel = route[:, R_AS:R_AS + 80]
                for t in range(NT):
                    out = ps[5][:, t * NE:(t + 1) * NE]
                    for s in range(t + 1):
                        T.matmul(out, C[:, K_UT:K_UT + P] if s == t else ones, sel[:, s * NE:(s + 1) * NE], start=s == 0, stop=s == t,
                                 skip_group_check=True)
                for s in range(NT):
                    ins = T.matmul(ps[5][:, 80:96], ones, sel[:, s * NE:(s + 1) * NE], start=s == 0, stop=s == NT - 1,
                                   skip_group_check=True)
                ins.then_inc(L["pos"], 1)
                for t in range(NT):
                    pe.wait_ge(L["oh"], t + 1)
                    for e in range(NE):
                        ins = T.matmul(ps[6][:, e:e + 1], oh[:, t % 2, e, :], tokf[:, t:t + 1], start=t == 0 and e == 0,
                                       stop=t == NT - 1, skip_group_check=True)
                    ins.then_inc(L["ohu"], 1)

                def uses(s):
                    return 3 if s < 4 else 2

                def step(i, u, head, tail):
                    e = i * 2 + u
                    s = 3 * u
                    pe.wait_ge(L["txa"], e + 1)
                    pe.wait_ge(L["txd"], e + 1)
                    came(s, uses(s) + i)
                    if not (head and u == 0):
                        pe.wait_ge(L["hid"], e)
                    gv = W[:, s, :].rearrange("p (k f) -> p k f", f=DE)
                    uv = W[:, s + 1, :].rearrange("p (k f) -> p k f", f=DE)
                    products(ps[2][:, 0:DE], [(xgT[:, u * KC + k, :], gv[:, k, :]) for k in range(KC)])
                    done_units.append(s)
                    came(s + 1, uses(s + 1) + i)
                    products(ps[2][:, DE:2 * DE], [(xgT[:, u * KC + k, :], uv[:, k, :]) for k in range(KC)], L["gu"])
                    done_units.append(s + 1)
                    if not (tail and u == 1):
                        un = 1 - u
                        pe.wait_ge(s_xg[un], (l * (NE // 2) + i + 1 + u) * 16)
                        for q in range(2):
                            turn([(ps[q][:, j * P:(j + 1) * P], xg[:, un, (4 * q + j) * P:(4 * q + j + 1) * P])
                                  for j in range(4)], L["tx"])
                    if not (head and u == 0):
                        down(i, u, e - 1, 1 - u, i - 1 + u, head and u == 1)
                    pe.wait_ge(L["hid"], e + 1)
                    turn([(ps[5][:, j * P:(j + 1) * P], hid[:, u, j * P:(j + 1) * P]) for j in range(2)], L["ht"])

                def down(i, u, e, par, use, first):
                    s = 3 * par + 2
                    pe.wait_ge(L["hta"], e + 1)
                    came(s, uses(s) + use)
                    dv = W[:, s, :].rearrange("p (k f) -> p k f", f=D)
                    for q in range(2):
                        if not first:
                            pe.wait_ge(L["ya" if q == 0 else "yd"], e)
                        products(ps[3 + q][:, :], [(hidT[:, 2 * par + k, :], dv[:, k, q * 512:(q + 1) * 512]) for k in range(2)],
                                 L["dn"])
                    done_units.append(s)

                pe.wait_ge(s_xg[0], l * (NE * 8) + 16)
                for q in range(2):
                    turn([(ps[q][:, j * P:(j + 1) * P], xg[:, 0, (4 * q + j) * P:(4 * q + j + 1) * P]) for j in range(4)], L["tx"])
                for u in range(2):
                    step(0, u, True, False)
                with pe.Fori(1, NE // 2 - 1) as i:
                    for u in range(2):
                        step(i, u, False, False)
                for u in range(2):
                    step(NE // 2 - 1, u, False, True)
                down(None, None, NE - 1, 1, NE // 2 - 1, False)

                while done_units:
                    T.transpose(ps[7][:, 0:128], ident, ident).then_inc(w_free[done_units.pop(0)], 1)
                pe.reg_add(n0, n0, 11)
                pe.reg_add(n3, n3, 11)
                pe.reg_add(n4, n4, 10)
                pe.wait_ge(L["ready"], 1)
                pe.reg_load(further, jobs[0:1, XJ:XJ + 1])
                with pe.If_ne(further, 0):
                    pe.wait_ge(L["ya"], NE)
                    pe.wait_ge(L["yd"], NE)
                    with pe.Fori(0, pe.snap(further, min_val=0, max_val=XJ)):
                        use = pe.snap(n0)
                        pe.wait_ge(M["oh"], 1)
                        products(ps[6][:, 0:1], [(ohx[:, k * NT + t, :], tokf[:, t:t + 1]) for k in range(2) for t in range(NT)], M["idx"])
                        pe.wait_ge(s_xx, pe.snap(gathers) * 16 + 16)
                        for q in range(2):
                            turn([(ps[q][:, j * P:(j + 1) * P], xg[:, 0, (4 * q + j) * P:(4 * q + j + 1) * P]) for j in range(4)], M["tx"])
                        pe.wait_ge(M["txa"], 1)
                        pe.wait_ge(M["txd"], 1)
                        for s in range(2):
                            pe.wait_ge(w_ld[s], use * 16 + 16)
                            wv = W[:, s, :].rearrange("p (k f) -> p k f", f=DE)
                            products(ps[2][:, s * DE:(s + 1) * DE], [(xgT[:, k, :], wv[:, k, :]) for k in range(KC)], M["gu"])
                        pe.wait_ge(M["hid"], 1)
                        turn([(ps[5][:, j * P:(j + 1) * P], hid[:, 0, j * P:(j + 1) * P]) for j in range(2)], M["ht"])
                        pe.wait_ge(M["hta"], 1)
                        pe.wait_ge(w_ld[2], use * 16 + 16)
                        dv = W[:, 2, :].rearrange("p (k f) -> p k f", f=D)
                        for q in range(2):
                            products(ps[3 + q][:, :], [(hidT[:, k, :], dv[:, k, q * 512:(q + 1) * 512]) for k in range(2)], M["dn"])
                        for s in range(3):
                            T.transpose(ps[7][:, 0:128], ident, ident).then_inc(w_free[s], 1)
                        pe.reg_add(n0, n0, 1)
                        pe.reg_add(gathers, gathers, 1)
                        leave(pe, "pe")
                leave(pe, "pe")

        @block.scalar
        def _(act):
            S = nc.scalar
            further = act.alloc_register("act_further")
            act.dma_start(C[:, :], A["consts"]).then_inc(s_c, 16)
            act.dma_start(srows[0:8, :], A["c_prompt"].rearrange("b (k p) -> (b k) p", p=P)).then_inc(s_r, 16)
            act.dma_start(srows[8:16, :], A["c_sample"].rearrange("b (k p) -> (b k) p", p=P)).then_inc(s_r, 16)
            act.dma_start(brows[0:96, :], A["b_ada"].rearrange("l (k p) -> (l k) p", p=P)).then_inc(s_x, 16)
            act.dma_start(X[:, 0:4, :], A["x_prompt"].rearrange("b (t p) d -> p (b t) d", p=P)).then_inc(s_x, 16)
            act.dma_start(X[0:DEC, 4, :], A["x_sample"][0]).then_inc(s_x, 16)
            act.wait_ge(s_r, 32)
            act.wait_ge(s_x, 48)
            S.activation(srows[0:16, :], srows[0:16, :], ACT.Silu).then_inc(s_silu, 1)
            act.wait_ge(s_mT, 2)
            for l in range(DEPTH):
                S.copy(mrow[0:96, l, :], ps[2 + l][0:96, 0:P]).then_inc(s_mTc, 1)
            act.wait_ge(s_mTc, 2)
            act.dma_start(mod_d.rearrange("l s q (k p) -> (s q k) l p", p=P), mrow[0:96, :, :]).then_inc(s_mst, 16)
            act.wait_ge(s_mst, 16)

            with act.Fori(0, DEPTH) as l:
                def at(name):
                    w = A[name][bass.ds(l, 1)]
                    return w

                ld = L["small_ld"]
                md = mod_d[bass.ds(l, 1)].rearrange("l s q (k p) -> s (l q k) p", p=P)
                act.dma_start(vrows[0:16, :], md[0, 0:16]).then_inc(ld, 16)
                act.dma_start(vrows[16:32, :], md[1, 0:16]).then_inc(ld, 16)
                act.dma_start(vrows[32:40, :], at("g_norm_mix").rearrange("l (k p) -> (l k) p", p=P)).then_inc(ld, 16)
                for n, name in enumerate(("conv_b", "ln_conv_g", "ln_conv_b")):
                    act.dma_start(vrows[40 + 4 * n:44 + 4 * n, :], at(name).rearrange("l (k p) -> (l k) p", p=P)).then_inc(ld, 16)
                act.dma_start(crows[0:31, :], at("conv_w").rearrange("l w c -> (l w) c")).then_inc(ld, 16)
                act.dma_start(crows[31:61, :], at("state_conv").rearrange("l b w c -> (l b w) c")).then_inc(ld, 16)
                act.dma_start(gq[:, 0, :], at("q_norm_g").broadcast_to([P, HD])).then_inc(ld, 16)
                act.dma_start(gq[:, 1, :], at("k_norm_g").broadcast_to([P, HD])).then_inc(ld, 16)
                act.dma_start(ck[:, :, :], at("cache_k").rearrange("l b (t p) n d -> p (l b t) (n d)", p=P)).then_inc(ld, 16)
                act.dma_start(cv[:, :, :], at("cache_v").rearrange("l b (t p) n d -> p (l b t) (n d)", p=P)).then_inc(ld, 16)
                for q in range(2):
                    act.dma_start(cik[:, :, 64 * q:64 * q + 64], at("cache_idx_k").rearrange("l b (t p) d -> p (l b t) d", p=P)).then_inc(ld, 16)
                act.dma_start(wr[:, :, 0:4], at("w_router_group").rearrange("l (k p) e -> p (l k) e", p=P)).then_inc(ld, 16)
                act.dma_start(wr[:, :, 4:20], at("w_router_expert").rearrange("l (k p) e -> p (l k) e", p=P)).then_inc(ld, 16)
                act.dma_start(rb[:, 0:4], at("b_router_group").broadcast_to([P, 4])).then_inc(ld, 16)
                act.dma_start(rb[:, 4:20], at("b_router_expert").broadcast_to([P, 16])).then_inc(ld, 16)
                mrows = mod_d[bass.ds(l, 1)].rearrange("l s q d -> s q l d")
                act.dma_start(gt[:, 0, :], mrows[0, 2].broadcast_to([P, D])).then_inc(L["gt_ld"], 16)
                act.dma_start(gt[0:DEC, 1, :], mrows[1, 2].broadcast_to([DEC, D])).then_inc(L["gt_ld"], 16)

                for t in range(NT):
                    m = rows_of(t)
                    if t >= 1:
                        act.wait_ge(L["sumsq"], t)
                    S.activation(junk[0:m], X[0:m, t, :], ACT.Square, accum_out=small[0:m, S_SS + t:S_SS + t + 1]).then_inc(L["sumsq"], 1)
                act.wait_ge(L["var"], 1)
                S.activation(small[:, S_RS:S_RS + 5], small[:, S_VAR:S_VAR + 5], ACT.Sqrt).then_inc(L["root"], 1)

                act.wait_ge(L["vecC"], 4)
                for k in range(0, KC, 2):
                    act.wait_ge(L["nT"], k + 1)
                    S.activation(hT[:, k, 0:SEQ], ps[k][:, :], ACT.Identity, bias=vT[:, k:k + 1],
                                 scale=small[:, S_AT + k:S_AT + k + 1]).then_inc(L["nTa"], 1)
                act.wait_ge(L["nT"], 9)
                for k in range(0, KC, 2):
                    S.activation(hT[:, k, SEQ:TOK], ps[0][:, k * DEC:(k + 1) * DEC], ACT.Identity, bias=vT[:, 16 + k:17 + k],
                                 scale=small[:, S_AT + 8 + k:S_AT + 9 + k]).then_inc(L["nTa"], 1)

                def out_of(job):
                    c, t = divmod(job, NT)
                    m = rows_of(t)
                    b = ps[job % 3]
                    act.wait_ge(L["proj"], job + 1)
                    if c == 0:
                        ins = S.copy(iqr[0:m, t, 0:8, :], b[0:m, :].rearrange("p (h d) -> p h d", d=HD))
                    elif c == 1:
                        for q in range(2):
                            S.copy(iqr[0:m, t, 8 + q, :], b[0:m, 0:HD])
                        ins = S.mul(iw[0:m, t, :], b[0:m, HD:HD + 8], IW_SCALE)
                    elif c == 2:
                        S.copy(qkf[0:m, t, 512:640], b[0:m, 0:P])
                        ins = S.copy(vrow[0:m, t, :], b[0:m, P:2 * P])
                    else:
                        ins = S.copy(qkr[0:m, t, 0:8, :].rearrange("p (i a) d -> p a i d", a=2),
                                     b[0:m, :].rearrange("p (a i d) -> p a i d", a=2, d=HD))
                    ins.then_inc(L["proja"], 1)
                for job in range(15):
                    out_of(job)

                def store(name, rows, src):
                    act.dma_start(rows(O[name][bass.ds(l, 1)]), src).then_inc(L["outst"], 16)

                def tiles(a):
                    return a.rearrange("l b (t p) n d -> p (l b t) (n d)", p=P)

                def row(a):
                    return a.rearrange("l b t n d -> (l b t) (n d)")
                act.wait_ge(L["proja"], 15)
                store("new_v_prompt", tiles, vrow[:, 0:4, :])
                store("new_v_sample", row, vrow[0:DEC, 4, :])
                act.wait_ge(L["ropei"], 2)
                store("new_idx_k_prompt", lambda a: a.rearrange("l b (t p) d -> p (l b t) d", p=P), iqf[:, 0:4, 512:576])
                store("new_idx_k_sample", lambda a: a.rearrange("l b t d -> (l b t) d"), iqf[0:DEC, 4, 512:576])

                def turned(job, keys):
                    for n in range(7):
                        act.wait_ge(L["tr"], job + n + 1)
                        b = ps[3 + n % 5]
                        if n < 4:
                            ins = S.copy(qT[:, n, 0:SEQ], b[:, :])
                        elif n == 4:
                            ins = S.copy(keys[:, 0:SEQ], b[:, :])
                        elif n == 5:
                            S.copy(qT[:, :, SEQ:TOK], b[:, 0:256].rearrange("p (i t) -> p i t", t=DEC))
                            ins = S.copy(keys[:, 1024:1088], b[:, 256:320])
                        else:
                            ins = S.copy(keys[:, SEQ:1024], b[:, :])
                        ins.then_inc(L["tra"], 1)
                act.wait_ge(s_init, 3)
                act.dma_start(y_d[XROW:XROW + XJ * P, :].rearrange("(p a) (b c) -> p (a b) c", p=P, c=256),
                              zeros[:, :].unsqueeze(1).to_broadcast([P, XJ * 4, 256])).then_inc(L["zst"], 16)
                turned(0, kT[0])
                for n, (t, h) in enumerate((t, h) for t in SCORED for h in range(8)):
                    m = rows_of(t)
                    a, b = keys_of(t)
                    act.wait_ge(L["dots"], n + 1)
                    if n >= 3:
                        act.wait_ge(L["score"], n - 2)
                    ins = S.activation(rel[0:m, n % 3, 0:b - a], ps[5 + n % 3][0:m, 0:b - a], ACT.Relu)
                    if t == 4:
                        ins = S.activation(rel[0:m, n % 3, 512:576], ps[3 + n % 2][0:m, 0:DEC], ACT.Relu)
                    ins.then_inc(L["rel"], 1)
                for job in range(15, 20):
                    out_of(job)
                act.wait_ge(L["proja"], 20)
                act.wait_ge(L["score"], 32)
                for t in range(NT):
                    m = rows_of(t)
                    S.activation(sq[0:m, t], qkr[0:m, t], ACT.Square).then_inc(L["sqd"], 1)

                def gates(i):
                    act.wait_ge(L["uproj"], 4 * i + 4)
                    if i == 0:
                        act.wait_ge(L["rel"], 32)
                    if i >= 2:
                        act.wait_ge(L["glup"], i - 1)
                    for ab, f in ((0, ACT.Copy), (1, ACT.Sigmoid)):
                        S.activation(glu[:, 2 * (i % 2) + ab, 0:SEQ], ps[3 + 2 * (i % 2) + ab][:, :], f)
                        ins = S.activation(glu[:, 2 * (i % 2) + ab, SEQ:TOK], ps[7 if i % 2 == 0 else 2][:, ab * DEC:(ab + 1) * DEC], f)
                    ins.then_inc(L["glua"], 1)
                gates(0)
                act.wait_ge(L["qvar"], 1)
                S.activation(small[:, S_QS + 50:S_QS + 100], small[:, S_QS:S_QS + 50], ACT.Sqrt).then_inc(L["qroot"], 1)
                for i in range(1, 4):
                    gates(i)
                act.wait_ge(L["ropeq"], 2)
                store("new_k_prompt", tiles, qkf[:, 0:4, 512:640])
                store("new_k_sample", row, qkf[0:DEC, 4, 512:640])
                turned(7, kT[1])
                for n in range(2):
                    act.wait_ge(L["cst"], n + 1)
                    S.copy(crows[32 * n:32 * n + 30, :], ps[6 + n][0:30, :]).then_inc(L["csta"], 1)
                act.wait_ge(L["csta"], 2)
                act.dma_start(O["new_conv_prompt"][bass.ds(l, 1)].rearrange("l b w c -> (l b w) c"), crows[0:30, :]).then_inc(L["outst"], 16)
                act.dma_start(O["new_conv_sample"][bass.ds(l, 1)].rearrange("l b w c -> (l b w) c"), crows[32:62, :]).then_inc(L["outst"], 16)

                def exps(n):
                    t, g = GROUPS[n]
                    m = rows_of(t)
                    act.wait_ge(L["nmx"], n + 1)
                    for i in range(4):
                        r = PR[0:m, 4 * (n % 2) + i, 0:NKEYS[t]]
                        h = S_SUM + 8 * ((n // 2) % 2) + 4 * g + i
                        q = S_NMX + 4 * (n % 2) + i
                        ins = S.activation(r, r, ACT.Exp, bias=small[0:m, q:q + 1], accum_out=small[0:m, h:h + 1])
                    ins.then_inc(L["pexp"], 1)

                def turned_output(tile, job):
                    m = rows_of(ATTN[tile])
                    act.wait_ge(L["pt"], job + 1)
                    t0 = ATTN[tile] * P
                    S.copy(hT[:, 0:4, t0:t0 + m], ps[4 + job % 2][:, 0:4 * m].rearrange("p (j t) -> p j t", j=4)).then_inc(L["pta"], 1)

                act.wait_ge(L["uproj"], 16)
                exps(0)
                exps(1)
                for n, (t, g) in enumerate(GROUPS):
                    m = rows_of(t)
                    if n >= 1:
                        act.wait_ge(L["pv"], n)
                    for q, (c, kn) in enumerate(chunks_of(t)):
                        job = TJ[n] + q
                        act.wait_ge(L["pt"], job + 1)
                        S.copy(pT[0:kn, c, 0:4 * m], ps[4 + job % 2][0:kn, 0:4 * m]).then_inc(L["pta"], 1)
                    if n + 2 < len(GROUPS):
                        if n % 2 == 0 and n >= 2:
                            act.wait_ge(L["on"], n // 2)
                        exps(n + 2)
                    if n >= 2 and n % 2 == 0:
                        turned_output(n // 2 - 1, TJ[n] + len(chunks_of(t)))
                turned_output(4, TJ[10])

                act.wait_ge(L["lnx"], 2)
                S.activation(sqc[:, :, 0:SEQ], cy[:, :, 0:SEQ], ACT.Square).then_inc(L["lnsq"], 1)
                S.activation(sqc[:, :, SEQ:TOK], cy[:, :, 542:606], ACT.Square).then_inc(L["lnsq"], 1)
                act.wait_ge(L["lnr"], 1)
                S.activation(lnb[:, :], lnb[:, :], ACT.Sqrt).then_inc(L["lnr"], 1)
                act.wait_ge(L["lny"], 2)
                for c in range(4):
                    for d, a, n in ((0, 0, SEQ), (SEQ, 542, DEC)):
                        S.activation(hT[:, 4 + c, d:d + n], cy[:, c, a:a + n], ACT.Silu, bias=vT[:, 48 + c:49 + c],
                                     scale=vT[:, 44 + c:45 + c]).then_inc(L["mixy"], 1)

                act.wait_ge(L["mixy"], 8)
                act.wait_ge(L["pta"], TJ[10] + 1)
                act.wait_ge(L["outst"], 16 * 8)
                for n, q in enumerate((4, 3)):
                    act.dma_start(AB[:, n, 0, :], mrows[0, q].broadcast_to([P, D])).then_inc(L["ab_ld"], 16)
                    act.dma_start(AB[0:DEC, n, 1, :], mrows[1, q].broadcast_to([DEC, D])).then_inc(L["ab_ld"], 16)
                act.dma_start(gf[:, :], A["g_norm_ffn"][bass.ds(l, 1)].broadcast_to([P, D])).then_inc(L["ab_ld"], 16)
                for t in range(NT):
                    m = rows_of(t)
                    act.wait_ge(L["xadd"], 6 + t)
                    if t >= 1:
                        act.wait_ge(L["fsum"], t)
                    S.activation(junk[0:m], X[0:m, t, :], ACT.Square, accum_out=small[0:m, S_FS + t:S_FS + t + 1]).then_inc(L["fsum"], 1)
                act.dma_start(gt[:, 0, :], mrows[0, 5].broadcast_to([P, D])).then_inc(L["gtf_ld"], 16)
                act.dma_start(gt[0:DEC, 1, :], mrows[1, 5].broadcast_to([DEC, D])).then_inc(L["gtf_ld"], 16)
                act.wait_ge(L["fvar"], 1)
                S.activation(small[:, S_FR:S_FR + 5], small[:, S_FV:S_FV + 5], ACT.Sqrt).then_inc(L["froot"], 1)
                for t in range(NT):
                    m = rows_of(t)
                    act.wait_ge(L["hrow"], t + 1)
                    act.dma_start(h_d[t * P:t * P + m, :], HR[0:m, t % 2, :]).then_inc(L[f"hst{t % 2}"], 16)
                    for q in range(2):
                        act.wait_ge(L["hTt"], 2 * t + q + 1)
                        S.copy(hT[:, 4 * q:4 * q + 4, t * P:t * P + m],
                               ps[2 * (t % 2) + q][:, 0:4 * m].rearrange("p (j t) -> p j t", j=4)).then_inc(L["hTa"], 1)
                act.wait_ge(L["gdiff"], 1)
                S.activation(route[:, R_GE:R_GE + 20], route[:, R_GE:R_GE + 20], ACT.Exp).then_inc(L["gexp"], 1)
                act.wait_ge(L["zdiff"], 1)
                S.activation(route[:, R_Z:R_Z + 5], route[:, R_Z:R_Z + 5], ACT.Exp).then_inc(L["zexp"], 1)

                act.wait_ge(L["ready"], 1)
                def turned_x(e, u):
                    act.wait_ge(L["tx"], e * 2 + 1)
                    S.copy(xgT[:, u * KC:u * KC + 4, :], ps[0][:, :].rearrange("p (j t) -> p j t", j=4)).then_inc(L["txa"], 1)

                def y_half(e, u):
                    act.wait_ge(L["dn"], e * 2 + 1)
                    S.copy(ys[:, u, 0:512], ps[3][:, :]).then_inc(L["ya"], 1)
                    act.wait_ge(L["yd"], e + 1)
                    act.wait_ge(L["ya"], e + 1)
                    act.dma_start(y_d[bass.ds(e * P, P), :], ys[:, u, :]).then_inc(L[f"yst{u}"], 16)

                def step(i, u, head, tail):
                    e = i * 2 + u
                    act.wait_ge(L["gu"], e + 1)
                    S.activation(sg[:, u, :], ps[2][:, 0:DE], ACT.Silu).then_inc(L["sg"], 1)
                    if not (tail and u == 1):
                        turned_x(e + 1, 1 - u)
                    if not (head and u == 0):
                        if not head and not (isinstance(i, int) and i - 1 + u == 0):
                            act.wait_ge(L[f"yst{1 - u}"], (i - 1 + u) * 16)
                        y_half(e - 1, 1 - u)
                    act.wait_ge(L["ht"], e + 1)
                    S.copy(hidT[:, 2 * u:2 * u + 2, :], ps[5][:, 0:256].rearrange("p (j t) -> p j t", j=2)).then_inc(L["hta"], 1)

                turned_x(0, 0)
                for u in range(2):
                    step(0, u, True, False)
                for u in range(2):
                    step(1, u, False, False)
                with act.Fori(2, NE // 2 - 1) as i:
                    for u in range(2):
                        step(i, u, False, False)
                for u in range(2):
                    step(NE // 2 - 1, u, False, True)
                act.wait_ge(L["yst1"], 16 * (NE // 2 - 1))
                y_half(NE - 1, 1)
                act.wait_ge(L["yst0"], 16 * (NE // 2))
                act.wait_ge(L["yst1"], 16 * (NE // 2))

                act.wait_ge(L["zst"], 16)
                act.reg_load(further, jobs[0:1, XJ:XJ + 1])
                with act.If_ne(further, 0):
                    with act.Fori(0, act.snap(further, min_val=0, max_val=XJ)) as x:
                        act.wait_ge(M["tx"], 1)
                        S.copy(xgT[:, 0:4, :], ps[0][:, :].rearrange("p (j t) -> p j t", j=4)).then_inc(M["txa"], 1)
                        act.wait_ge(M["gu"], 2)
                        S.activation(sg[:, 0, :], ps[2][:, 0:DE], ACT.Silu).then_inc(M["sg"], 1)
                        act.wait_ge(M["ht"], 1)
                        S.copy(hidT[:, 0:2, :], ps[5][:, 0:256].rearrange("p (j t) -> p j t", j=2)).then_inc(M["hta"], 1)
                        act.wait_ge(M["dn"], 1)
                        S.copy(ys[:, 0, 0:512], ps[3][:, :]).then_inc(M["ya"], 1)
                        act.wait_ge(M["ya"], 1)
                        act.wait_ge(M["yd"], 1)
                        act.dma_start(y_d[bass.ds(x * P + XROW, P), :], ys[:, 0, :]).then_inc(M["yst"], 16)
                        act.wait_ge(M["yst"], 16)
                        leave(act, "act")
                leave(act, "act")
            act.wait_ge(s_fin, 1)
            act.dma_start(O["y_prompt"].rearrange("b (t p) d -> p (b t) d", p=P), X[:, 0:4, :]).then_inc(y_out, 16)
            act.dma_start(O["y_sample"][0], X[0:DEC, 4, :]).then_inc(y_out, 16)
            act.wait_ge(y_out, 32)

        @block.vector
        def _(dve):
            V = nc.vector
            further = dve.alloc_register("dve_further")
            V.memset(small[:, :], 1.0).then_inc(s_init, 1)
            V.memset(zeros[:, :], 0.0).then_inc(s_init, 1)
            dve.sem_inc(s_adae, 2)
            dve.wait_ge(s_c, 16)
            V.tensor_copy(tokf[:, :], C[:, K_TOK:K_TOK + NT]).then_inc(s_init, 1)
            dve.wait_ge(s_cT, 1)
            V.tensor_copy(scT[:, :, :], ps[7][:, 0:16].rearrange("p (s k) -> p s k", s=2)).then_inc(s_cTc, 1)
            V.tensor_copy(baT[:, :], ps[7][:, 128:224]).then_inc(s_cTc, 1)
            dve.wait_ge(s_cTc, 2)
            with dve.Fori(0, DEPTH) as l:
                with dve.Fori(0, 2) as h:
                    for u in range(2):
                        at = l * 96 + h * 24 + u * 12
                        dve.wait_ge(s_ada, l * 4 + h * 2 + u + 1)
                        for st in range(2):
                            ins = V.tensor_tensor(modf[:, bass.ds(at + 48 * st, 12)], ps[u][:, 0:24].rearrange("p (j s) -> p j s", s=2)[:, :, st],
                                                  baT[:, bass.ds(l * 48 + h * 24 + u * 12, 12)], ALU.add)
                        ins.then_inc(s_adae, 1)
            dve.wait_ge(s_init, 3)
            dve.wait_ge(s_x, 48)

            with dve.Fori(0, DEPTH) as l:
                n_chain = [0]

                def chain(ins):
                    n_chain[0] += 1
                    ins.then_inc(L["dch"], 1)
                    dve.wait_ge(L["dch"], n_chain[0])

                dve.wait_ge(L["vecT"], 2)
                V.tensor_copy(vT[:, :], ps[6][:, 0:52]).then_inc(L["vecC"], 1)
                cr = ps[7][:, 0:244].rearrange("p (c w) -> p c w", w=61)
                V.tensor_copy(taps[:, :, :], cr[:, :, 0:CW]).then_inc(L["vecC"], 1)
                V.tensor_copy(gT[:, :, 542:572], cr[:, :, CW:61]).then_inc(L["vecC"], 1)
                dve.wait_ge(L["vecC"], 3)
                V.scalar_tensor_tensor(small[:, S_AT:S_AT + 16].rearrange("p (s k) -> p s k", s=2),
                                       vT[:, 0:32].rearrange("p (s q k) -> p s q k", s=2, q=2)[:, :, 1, :], 1.0,
                                       vT[:, 32:40].unsqueeze(1).to_broadcast([P, 2, KC]), ALU.add, ALU.mult).then_inc(L["vecC"], 1)

                def inverse(sums, var, root, n, scale, s_in, n_in, s_var, s_root):
                    dve.wait_ge(s_in, n_in)
                    V.tensor_scalar(small[:, var:var + n], small[:, sums:sums + n], scale, EPS, ALU.mult, ALU.add).then_inc(s_var, 1)
                    dve.wait_ge(s_root, 1)
                    chain(V.reciprocal(small[:, root:root + n], small[:, root:root + n]))

                inverse(S_SS, S_VAR, S_RS, 5, 1.0 / D, L["sumsq"], NT, L["var"], L["root"])
                for t in range(NT):
                    m = rows_of(t)
                    V.tensor_scalar(XN[0:m, t, :], X[0:m, t, :], small[0:m, S_RS + t:S_RS + t + 1], None, ALU.mult).then_inc(L["xn"], 1)
                dve.wait_ge(L["vecC"], 4)
                for k in range(1, KC, 2):
                    dve.wait_ge(L["nT"], k + 1)
                    V.tensor_scalar(hT[:, k, 0:SEQ], ps[k][:, :], small[:, S_AT + k:S_AT + k + 1], vT[:, k:k + 1],
                                    ALU.mult, ALU.add).then_inc(L["nTd"], 1)
                dve.wait_ge(L["nT"], 10)
                for k in range(1, KC, 2):
                    V.tensor_scalar(hT[:, k, SEQ:TOK], ps[1][:, k * DEC:(k + 1) * DEC], small[:, S_AT + 8 + k:S_AT + 9 + k],
                                    vT[:, 16 + k:17 + k], ALU.mult, ALU.add).then_inc(L["nTd"], 1)

                dve.wait_ge(L["proja"], 10)
                for r, t0, t1 in PARTS:
                    rope(dve, V, iqr, r, t0, t1, 16880, L["dch"], n_chain, L["ropei"])

                for n, (t, h) in enumerate((t, h) for t in SCORED for h in range(8)):
                    m = rows_of(t)
                    sc = msk[0:m, MSK_AT[t]:MSK_AT[t] + NKEYS[t]]
                    dve.wait_ge(L["rel"], n + 1)
                    w = iw[0:m, t, h:h + 1]
                    if h == 0:
                        V.tensor_scalar(sc, rel[0:m, n % 3, 0:NKEYS[t]], w, None, ALU.mult).then_inc(L["score"], 1)
                    else:
                        dve.wait_ge(L["score"], n)
                        V.scalar_tensor_tensor(sc, rel[0:m, n % 3, 0:NKEYS[t]], w, sc, ALU.mult, ALU.add).then_inc(L["score"], 1)
                dve.wait_ge(L["score"], 32)

                def select(t):
                    m, n = rows_of(t), NKEYS[t]
                    sc = msk[0:m, MSK_AT[t]:MSK_AT[t] + n]
                    m8 = small[0:m, S_M8:S_M8 + 8]
                    if t < 4:
                        chain(V.memset(sc[0:64, n - 64:n], -BIG))
                    for _ in range(TOPK[t] // 8):
                        chain(V.max(m8, sc))
                        chain(V.match_replace(sc, m8, sc, MARK))
                    chain(V.tensor_scalar(sc, sc, MARK, -BIG, ALU.not_equal, ALU.mult))

                select(4)
                select(3)
                dve.wait_ge(L["sqd"], NT)
                for r, t0, t1 in PARTS:
                    o = small[0:r, S_QS + 10 * t0:S_QS + 10 * t1]
                    chain(V.tensor_reduce(o.rearrange("p (t h) -> p t h", h=10), sq[0:r, t0:t1], AX.X, ALU.add))
                V.tensor_scalar(small[:, S_QS:S_QS + 50], small[:, S_QS:S_QS + 50], 1.0 / HD, EPS, ALU.mult, ALU.add).then_inc(L["qvar"], 1)
                select(2)
                dve.wait_ge(L["qroot"], 1)
                V.reciprocal(small[:, S_QS + 50:S_QS + 100], small[:, S_QS + 50:S_QS + 100]).then_inc(L["qinv"], 1)
                select(1)

                taps_done = [0]
                dve.wait_ge(L["glup"], 4)

                def conv(steps):
                    for _ in range(steps):
                        n = taps_done[0]
                        if n >= NCDVE:
                            return
                        w, c = divmod(n, DVE_CONV)
                        g = gT[:, c, w:w + 606]
                        if w == 0:
                            V.tensor_scalar(cy[:, c, :], g, taps[:, c, 0:1], vT[:, 40 + c:41 + c], ALU.mult, ALU.add).then_inc(L["cdve"], 1)
                        else:
                            dve.wait_ge(L["cdve"], n - DVE_CONV + 1)
                            V.scalar_tensor_tensor(cy[:, c, :], g, taps[:, c, w:w + 1], cy[:, c, :], ALU.mult, ALU.add).then_inc(L["cdve"], 1)
                        taps_done[0] += 1

                def masked(n):
                    t, g = GROUPS[n]
                    m = rows_of(t)
                    mk = C[0:m, K_M0:K_M0 + P] if t == 0 else msk[0:m, MSK_AT[t]:MSK_AT[t] + NKEYS[t]]
                    if n >= 2:
                        dve.wait_ge(L["pt"], TJ[n - 2] + len(chunks_of(GROUPS[n - 2][0])))
                    for i in range(4):
                        job = 4 * n + i
                        dve.wait_ge(L["lgt"], job + 1)
                        r = PR[0:m, 4 * (n % 2) + i, :]
                        k = min(NKEYS[t], 512)
                        mx = S_MX + i
                        ins = V.tensor_tensor_reduce(r[:, 0:k], ps[logit_bank(job)][0:m, 0:k], mk[:, 0:k], 0.125, MARK, ALU.add, ALU.max,
                                                     small[0:m, mx:mx + 1])
                        if t == 4:
                            ins = V.tensor_tensor_reduce(r[:, 512:576], ps[2 + job % 2][0:m, 0:DEC], mk[:, 512:576], 0.125, MARK,
                                                         ALU.add, ALU.max, small[0:m, mx + 4:mx + 5])
                        ins.then_inc(L["ttr"], 1)
                    dve.wait_ge(L["ttr"], 4 * n + 4)
                    if t == 4:
                        chain(V.tensor_tensor(small[0:m, S_MX:S_MX + 4], small[0:m, S_MX:S_MX + 4], small[0:m, S_MX + 4:S_MX + 8], ALU.max))
                    if n >= 2:
                        dve.wait_ge(L["pexp"], n - 1)
                    q = S_NMX + 4 * (n % 2)
                    V.tensor_scalar(small[0:m, q:q + 4], small[0:m, S_MX:S_MX + 4], -1.0, None, ALU.mult).then_inc(L["nmx"], 1)
                    dve.wait_ge(L["nmx"], n + 1)

                def normalize(tile):
                    m = rows_of(ATTN[tile])
                    dve.wait_ge(L["pv"], 2 * tile + 2)
                    s = S_SUM + 8 * (tile % 2)
                    chain(V.reciprocal(small[0:m, S_INV:S_INV + 8], small[0:m, s:s + 8]))
                    if tile >= 1:
                        dve.wait_ge(L["pt"], TJ[2 * tile] + len(chunks_of(ATTN[tile])) + 1)
                    V.tensor_tensor(orow[0:m].rearrange("p (h d) -> p h d", d=HD), ps[6 + tile % 2][0:m, :].rearrange("p (h d) -> p h d", d=HD),
                                    small[0:m, S_INV:S_INV + 8].unsqueeze(2).to_broadcast([m, 8, HD]), ALU.mult).then_inc(L["on"], 1)

                dve.wait_ge(L["ropeq"], 2)
                masked(0)
                masked(1)
                for n in range(len(GROUPS)):
                    if n + 2 < len(GROUPS):
                        masked(n + 2)
                    if n % 2 == 0 and n >= 2:
                        normalize(n // 2 - 1)
                    conv(10)
                normalize(4)
                conv(NCDVE)

                dve.wait_ge(L["lnm"], 2)
                dve.wait_ge(L["cdve"], NCDVE)
                for n, (b, a, w) in enumerate(((0, 0, SEQ), (1, 542, DEC))):
                    for c in range(4):
                        ins = V.scalar_tensor_tensor(cy[:, c, a:a + w], ps[b][:, 0:w], -1.0 / 512, cy[:, c, a:a + w], ALU.mult, ALU.add)
                    ins.then_inc(L["lnx"], 1)
                dve.wait_ge(L["lnv"], 2)
                V.tensor_scalar(lnb[:, 0:SEQ], ps[2][:, :], 1.0 / 512, EPS, ALU.mult, ALU.add)
                V.tensor_scalar(lnb[:, SEQ:TOK], ps[3][:, 0:DEC], 1.0 / 512, EPS, ALU.mult, ALU.add).then_inc(L["lnr"], 1)
                dve.wait_ge(L["lnr"], 2)
                chain(V.reciprocal(lnb[:, :], lnb[:, :]))
                dve.wait_ge(L["lnx"], 2)
                for a, s, w in ((0, 0, SEQ), (542, SEQ, DEC)):
                    V.tensor_tensor(cy[:, :, a:a + w], cy[:, :, a:a + w], lnb[:, s:s + w].unsqueeze(1).to_broadcast([P, 4, w]),
                                    ALU.mult).then_inc(L["lny"], 1)

                dve.wait_ge(L["gt_ld"], 32)
                for n in range(10):
                    t, hf = n % NT, n // NT
                    m = rows_of(t)
                    dve.wait_ge(L["wo"], n + 1)
                    if n >= 2:
                        dve.wait_ge(L["xadd"], n - 1)
                    V.tensor_tensor(wtmp[0:m, n % 2, :], ps[4 + n % 4][0:m, :], gt[0:m, t // 4, hf * 512:hf * 512 + 512],
                                    ALU.mult).then_inc(L["wod"], 1)

                dve.wait_ge(L["ab_ld"], 80)
                for s in range(2):
                    m = P if s == 0 else DEC
                    chain(V.scalar_tensor_tensor(AB[0:m, 0, s, :], AB[0:m, 0, s, :], 1.0, gf[0:m, :], ALU.add, ALU.mult))
                inverse(S_FS, S_FV, S_FR, 5, 1.0 / D, L["fsum"], NT, L["fvar"], L["froot"])
                for t in range(NT):
                    m = rows_of(t)
                    if t >= 2:
                        dve.wait_ge(L[f"hst{t % 2}"], 16 * (t // 2))
                        dve.wait_ge(L["hTt"], 2 * (t - 1))
                    hr = HR[0:m, t % 2, :]
                    chain(V.scalar_tensor_tensor(hr, X[0:m, t, :], small[0:m, S_FR + t:S_FR + t + 1], AB[0:m, 0, t // 4, :], ALU.mult, ALU.mult))
                    V.tensor_tensor(hr, hr, AB[0:m, 1, t // 4, :], ALU.add).then_inc(L["hrow"], 1)

                def R(at, *shape):
                    n = int(np.prod(shape))
                    v = route[:, at:at + n]
                    return v.rearrange("p (t e) -> p t e", t=shape[0]) if len(shape) == 2 else v

                def wide(v, n):
                    return v.unsqueeze(2).to_broadcast([P, NT, n])

                def iota(n):
                    return C[:, K_E16:K_E16 + n].unsqueeze(1).to_broadcast([P, NT, n])

                def first_largest(v, n, big, eq, least, onehot):
                    chain(V.tensor_reduce(big, v, AX.X, ALU.max))
                    chain(V.tensor_tensor(eq, v, wide(big, n), ALU.is_equal))
                    chain(V.scalar_tensor_tensor(eq, eq, -100.0, iota(n), ALU.mult, ALU.add))
                    chain(V.tensor_reduce(least, eq, AX.X, ALU.min))
                    chain(V.tensor_tensor(onehot, eq, wide(least, n), ALU.is_equal))

                lg = R(R_LG, NT, 20)
                chain(V.memset(lg[64:128, 4, :], 0.0))
                dve.wait_ge(L["rl"], NT)
                for r, t0, t1 in PARTS:
                    chain(V.tensor_tensor(lg[0:r, t0:t1], ps[4][0:r, t0 * 20:t1 * 20].rearrange("p (t e) -> p t e", e=20),
                                          rb[0:r, :].unsqueeze(1).to_broadcast([r, t1 - t0, 20]), ALU.add))
                goh, em = R(R_GOH, NT, 4), R(R_EM, NT, NE)
                oh1, oh2 = R(R_OH1, NT, NE), R(R_OH2, NT, NE)
                first_largest(lg[:, :, 0:4], 4, R(R_GM, NT), R(R_EQ, NT, 4), R(R_MI, NT), goh)
                V.tensor_tensor(R(R_GE, NT, 4), lg[:, :, 0:4], wide(R(R_GM, NT), 4), ALU.subtract).then_inc(L["gdiff"], 1)
                chain(V.tensor_scalar(R(R_W, NT, 4), goh, 1.0, BIG, ALU.subtract, ALU.mult))
                for g in range(4):
                    V.tensor_tensor(em[:, :, 4 * g:4 * g + 4], lg[:, :, 4 + 4 * g:8 + 4 * g],
                                    wide(R(R_W, NT, 4)[:, :, g], 4), ALU.add)
                chain(V.memset(R(R_TMP, NT, NE), 0.0))
                chain(V.tensor_scalar(em, em, 1.0, None, ALU.mult))
                first_largest(em, NE, R(R_M1, NT), R(R_EQ1, NT, NE), R(R_MI1, NT), oh1)
                chain(V.scalar_tensor_tensor(em, oh1, -BIG, em, ALU.mult, ALU.add))
                first_largest(em, NE, R(R_M2, NT), R(R_EQ1, NT, NE), R(R_MI1, NT), oh2)
                V.tensor_tensor(R(R_Z, NT), R(R_M2, NT), R(R_M1, NT), ALU.subtract).then_inc(L["zdiff"], 1)
                chain(V.memset(oh1[64:128, 4, :], 0.0))
                chain(V.memset(oh2[64:128, 4, :], 0.0))
                V.tensor_tensor(R(R_AS, NT, NE), oh1, oh2, ALU.add).then_inc(L["assign"], 1)
                dve.wait_ge(L["gexp"], 1)
                chain(V.tensor_reduce(R(R_PG, NT), R(R_GE, NT, 4), AX.X, ALU.add))
                dve.wait_ge(L["zexp"], 1)
                chain(V.tensor_scalar(R(R_G2, NT), R(R_Z, NT), 1.0, None, ALU.add))
                chain(V.tensor_tensor(R(R_G1, NT), R(R_G2, NT), R(R_PG, NT), ALU.mult))
                chain(V.reciprocal(R(R_G1, NT), R(R_G1, NT)))
                chain(V.tensor_tensor(R(R_G2, NT), R(R_G1, NT), R(R_Z, NT), ALU.mult))
                dve.wait_ge(L["pos"], 1)
                dve.wait_ge(L["assign"], 1)
                place = ps[5][:, 0:80].rearrange("p (t e) -> p t e", e=NE)
                exceeds = R(R_EQ1, 4 * NE).rearrange("p (q e) -> p q e", e=NE)
                for q in range(4):
                    ins = V.tensor_scalar(exceeds[:, q, :], ps[5][:, 80:96], P * (q + 1.0), None, ALU.is_gt)
                chain(ins)
                sums = R(R_EM, 3 * NE)
                own, odd, even = sums[:, 0:NE], sums[:, NE:2 * NE], sums[:, 2 * NE:3 * NE]
                chain(V.tensor_reduce(own, exceeds.rearrange("p q e -> p e q"), AX.X, ALU.add))
                src = own
                for n, d in enumerate((1, 2, 4, 8)):
                    dst = odd if n % 2 == 0 else even
                    V.tensor_copy(dst[:, 0:d], src[:, 0:d])
                    chain(V.tensor_tensor(dst[:, d:NE], src[:, d:NE], src[:, 0:NE - d], ALU.add))
                    src = dst
                incl = src
                before = R(R_POS, XJ * NE).rearrange("p (j e) -> p j e", e=NE)
                expert = R(R_LG, XJ + 1)
                chain(V.tensor_tensor(before, incl.unsqueeze(1).to_broadcast([P, XJ, NE]),
                                      C[:, K_E16:K_E16 + XJ].unsqueeze(2).to_broadcast([P, XJ, NE]), ALU.is_le))
                V.tensor_reduce(expert[:, 0:XJ], before, AX.X, ALU.add)
                chain(V.tensor_copy(expert[:, XJ:XJ + 1], incl[:, NE - 1:NE]))
                V.tensor_copy(jobs[:, :], expert).then_inc(L["dch"], 1)
                n_chain[0] += 1
                chain(V.tensor_tensor(own, incl, own, ALU.subtract))
                chain(V.tensor_scalar(own, own, float(P), float(XROW - P), ALU.mult, ALU.add))
                chain(V.tensor_tensor(own, own, C[:, K_ROW:K_ROW + NE], ALU.subtract))
                pos, tmp = R(R_POS, NT, NE), R(R_TMP, NT, NE)
                chain(V.scalar_tensor_tensor(tmp, place, P - 0.5, own.unsqueeze(1).to_broadcast([P, NT, NE]), ALU.is_gt, ALU.mult))
                chain(V.tensor_tensor(tmp, tmp, place, ALU.add))
                chain(V.tensor_tensor(tmp, tmp, C[:, K_ROW:K_ROW + NE].unsqueeze(1).to_broadcast([P, NT, NE]), ALU.add))
                for k, o in enumerate((oh1, oh2)):
                    chain(V.tensor_tensor(pos, tmp, o, ALU.mult))
                    chain(V.tensor_reduce(R(R_S + 5 * k, NT), pos, AX.X, ALU.add))
                chain(V.tensor_copy(sid[:, :], R(R_S, 2 * NT)))
                chain(V.scalar_tensor_tensor(pos, place, 1.0, R(R_AS, NT, NE), ALU.add, ALU.mult))
                chain(V.tensor_scalar(pos, pos, -1.0, None, ALU.add))
                dve.sem_inc(n_cnt, 1)
                dve.sem_inc(L["ready"], 1)

                for t in range(NT):
                    if t >= 2:
                        dve.wait_ge(L["ohu"], t - 1)
                    V.tensor_tensor(oh[:, t % 2], C[:, K_IOTA:K_IOTA + P].unsqueeze(1).to_broadcast([P, NE, P]),
                                    pos[:, t, :].unsqueeze(2).to_broadcast([P, NE, P]), ALU.is_equal).then_inc(L["oh"], 1)
                dve.wait_ge(L["ohu"], NT)
                V.tensor_copy(idx[:, 0:NE], ps[6][:, 0:NE]).then_inc(L["idx"], 1)

                def turned_x(e, u):
                    dve.wait_ge(L["tx"], e * 2 + 2)
                    V.tensor_copy(xgT[:, u * KC + 4:u * KC + 8, :], ps[1][:, :].rearrange("p (j t) -> p j t", j=4)).then_inc(L["txd"], 1)

                def y_half(e, u):
                    dve.wait_ge(L["dn"], e * 2 + 2)
                    V.tensor_copy(ys[:, u, 512:1024], ps[4][:, :]).then_inc(L["yd"], 1)

                def step(i, u, head, tail):
                    e = i * 2 + u
                    dve.wait_ge(L["sg"], e + 1)
                    V.tensor_tensor(hid[:, u, :], sg[:, u, :], ps[2][:, DE:2 * DE], ALU.mult).then_inc(L["hid"], 1)
                    if not (tail and u == 1):
                        turned_x(e + 1, 1 - u)
                    if not (head and u == 0):
                        if not head and not (isinstance(i, int) and i - 1 + u == 0):
                            dve.wait_ge(L[f"yst{1 - u}"], (i - 1 + u) * 16)
                        y_half(e - 1, 1 - u)

                turned_x(0, 0)
                for u in range(2):
                    step(0, u, True, False)
                for u in range(2):
                    step(1, u, False, False)
                with dve.Fori(2, NE // 2 - 1) as i:
                    for u in range(2):
                        step(i, u, False, False)
                for u in range(2):
                    step(NE // 2 - 1, u, False, True)
                dve.wait_ge(L["yst1"], 16 * (NE // 2 - 1))
                y_half(NE - 1, 1)
                xrow = R(R_TMP, 2 * NT)
                chain(V.tensor_scalar(xrow, R(R_S, 2 * NT), -float(XROW), None, ALU.add))
                dve.reg_load(further, jobs[0:1, XJ:XJ + 1])
                with dve.If_ne(further, 0):
                    with dve.Fori(0, dve.snap(further, min_val=0, max_val=XJ)):
                        V.tensor_tensor(ohx[:, :, :], C[:, K_IOTA:K_IOTA + P].unsqueeze(1).to_broadcast([P, 2 * NT, P]),
                                        xrow.unsqueeze(2).to_broadcast([P, 2 * NT, P]), ALU.is_equal).then_inc(M["oh"], 1)
                        dve.wait_ge(M["idx"], 1)
                        V.tensor_copy(idx[:, NE:NE + 1], ps[6][:, 0:1]).then_inc(M["idc"], 1)
                        dve.wait_ge(M["tx"], 2)
                        V.tensor_copy(xgT[:, 4:8, :], ps[1][:, :].rearrange("p (j t) -> p j t", j=4)).then_inc(M["txd"], 1)
                        dve.wait_ge(M["sg"], 1)
                        V.tensor_tensor(hid[:, 0, :], sg[:, 0, :], ps[2][:, DE:2 * DE], ALU.mult).then_inc(M["hid"], 1)
                        dve.wait_ge(M["dn"], 2)
                        dve.wait_ge(L["yst0"], 16 * (NE // 2))
                        V.tensor_copy(ys[:, 0, 512:1024], ps[4][:, :]).then_inc(M["yd"], 1)
                        dve.wait_ge(M["oh"], 1)
                        V.tensor_scalar(xrow, xrow, -float(P), None, ALU.add).then_inc(M["rch"], 1)
                        dve.wait_ge(M["rch"], 1)
                        release(dve, mrange)

                dve.wait_ge(L["gtf_ld"], 32)
                for t in range(NT):
                    m = rows_of(t)
                    dve.wait_ge(s_yg[t % 2], l * (96 if t % 2 == 0 else 64) + 32 * (t // 2 + 1))
                    y1, y2 = yg[0:m, 2 * (t % 2), :], yg[0:m, 2 * (t % 2) + 1, :]
                    chain(V.tensor_scalar(y1, y1, route[0:m, R_G1 + t:R_G1 + t + 1], None, ALU.mult))
                    chain(V.scalar_tensor_tensor(y1, y2, route[0:m, R_G2 + t:R_G2 + t + 1], y1, ALU.mult, ALU.add))
                    chain(V.tensor_tensor(y1, y1, gt[0:m, t // 4, :], ALU.mult))
                    V.tensor_tensor(X[0:m, t, :], X[0:m, t, :], y1, ALU.add).then_inc(L["comb"], 1)
                dve.wait_ge(L["comb"], NT)
                release(dve, lrange)
            dve.sem_inc(s_fin, 1)

        @block.gpsimd
        def _(pool):
            G = nc.gpsimd
            further = pool.alloc_register("pool_further")
            with pool.Fori(0, DEPTH) as l:
                n_chain = [0]

                def chain(ins):
                    n_chain[0] += 1
                    ins.then_inc(L["pch"], 1)
                    pool.wait_ge(L["pch"], n_chain[0])

                chain(G.memset(gT[:, :, 0:30], 0.0))

                def multiply(i):
                    pool.wait_ge(L["glua"], i + 1)
                    s = 2 * (i % 2)
                    G.tensor_tensor(gT[:, i, 30:542], glu[:, s, 0:SEQ], glu[:, s + 1, 0:SEQ], ALU.mult)
                    G.tensor_tensor(gT[:, i, 572:636], glu[:, s, SEQ:TOK], glu[:, s + 1, SEQ:TOK], ALU.mult).then_inc(L["glup"], 1)
                multiply(0)
                pool.wait_ge(L["qinv"], 1)
                pool.wait_ge(L["outst"], 64)
                for r, t0, t1 in PARTS:
                    inv = small[0:r, S_QS + 50 + 10 * t0:S_QS + 50 + 10 * t1].rearrange("p (t h) -> p t h", h=10)
                    v = qkr[0:r, t0:t1]
                    chain(G.tensor_tensor(v, v, inv.unsqueeze(3).to_broadcast([r, t1 - t0, 10, HD]), ALU.mult))
                    for a, b, j in ((0, 8, 0), (8, 10, 1)):
                        v = qkr[0:r, t0:t1, a:b, :]
                        chain(G.tensor_tensor(v, v, gq[0:r, j, :].unsqueeze(1).unsqueeze(1).to_broadcast([r, t1 - t0, b - a, HD]), ALU.mult))
                    rope(pool, G, qkr, r, t0, t1, 0, L["pch"], n_chain, L["ropeq"])
                for i in range(1, 4):
                    multiply(i)
                pool.wait_ge(L["glup"], 4)
                pool.wait_ge(L["vecC"], 4)
                for w in range(CW):
                    for c in range(DVE_CONV, 4):
                        g = gT[:, c, w:w + 606]
                        if w == 0:
                            G.tensor_scalar(cy[:, c, :], g, taps[:, c, 0:1], vT[:, 40 + c:41 + c], ALU.mult, ALU.add).then_inc(L["cpool"], 1)
                        else:
                            n = w * (4 - DVE_CONV) + c - DVE_CONV
                            pool.wait_ge(L["cpool"], max(n - 1, 1))
                            chain(G.tensor_scalar(ctmp[:, n % 2, :], g, taps[:, c, w:w + 1], None, ALU.mult))
                            pool.wait_ge(L["cpool"], n - 4 + DVE_CONV + 1)
                            G.tensor_tensor(cy[:, c, :], cy[:, c, :], ctmp[:, n % 2, :], ALU.add).then_inc(L["cpool"], 1)
                for n in range(10):
                    t, hf = n % NT, n // NT
                    m = rows_of(t)
                    pool.wait_ge(L["wod"], n + 1)
                    xs = X[0:m, t, hf * 512:hf * 512 + 512]
                    G.tensor_tensor(xs, xs, wtmp[0:m, n % 2, :], ALU.add).then_inc(L["xadd"], 1)
                pool.wait_ge(L["ready"], 1)
                pool.wait_ge(L["hst0"], 48)
                pool.wait_ge(L["hst1"], 32)
                pool.wait_ge(L["idx"], 1)
                for e in range(NE):
                    if e >= 2:
                        pool.wait_ge(L["tx"], 2 * (e - 1))
                    G.indirect_dma_start(out=xg[:, e % 2, :], out_offset=None, in_=h_d[:, :],
                                         in_offset=bass.IndirectOffsetOnAxis(ap=idx[:, e:e + 1], axis=0)).then_inc(s_xg[e % 2], 16)
                pool.wait_ge(L["tx"], 2 * NE)
                pool.reg_load(further, jobs[0:1, XJ:XJ + 1])
                with pool.If_ne(further, 0):
                    with pool.Fori(0, pool.snap(further, min_val=0, max_val=XJ)):
                        pool.wait_ge(M["idc"], 1)
                        G.indirect_dma_start(out=xg[:, 0, :], out_offset=None, in_=h_d[:, :],
                                             in_offset=bass.IndirectOffsetOnAxis(ap=idx[:, NE:NE + 1], axis=0)).then_inc(s_xx, 16)
                        leave(pool, "pool")
                pool.wait_ge(L["yst0"], 16 * (NE // 2))
                pool.wait_ge(L["yst1"], 16 * (NE // 2))
                pool.wait_ge(L["zst"], 16)
                for t in range(NT):
                    m = rows_of(t)
                    if t >= 2:
                        pool.wait_ge(L["comb"], t - 1)
                    for k in range(2):
                        G.indirect_dma_start(out=yg[0:m, 2 * (t % 2) + k, :], out_offset=None, in_=y_d[:, :],
                                             in_offset=bass.IndirectOffsetOnAxis(ap=sid[0:m, 5 * k + t:5 * k + t + 1], axis=0)
                                             ).then_inc(s_yg[t % 2], 16)
                leave(pool, "pool")


_INS = ["x_prompt", "x_sample", "c_prompt", "c_sample", "cache_k", "cache_v", "cache_idx_k", "state_conv",
        "w_ada", "b_ada", "g_norm_mix", "w_in", "q_norm_g", "k_norm_g", "conv_w", "conv_b", "ln_conv_g", "ln_conv_b",
        "w_out", "g_norm_ffn", "w_router_group", "b_router_group", "w_router_expert", "b_router_expert",
        "w_gate", "w_up", "w_down"]
_OUTS = [("y_prompt", (1, SEQ, D)), ("y_sample", (1, DEC, D)),
         ("new_k_prompt", (DEPTH, 1, SEQ, 2, HD)), ("new_v_prompt", (DEPTH, 1, SEQ, 2, HD)),
         ("new_idx_k_prompt", (DEPTH, 1, SEQ, HD)), ("new_conv_prompt", (DEPTH, 1, CW - 1, 512)),
         ("new_k_sample", (DEPTH, 1, DEC, 2, HD)), ("new_v_sample", (DEPTH, 1, DEC, 2, HD)),
         ("new_idx_k_sample", (DEPTH, 1, DEC, HD)), ("new_conv_sample", (DEPTH, 1, CW - 1, 512))]


def kernel(**inputs):
    import concourse.bacc as _bacc
    from concourse.bass_utils import run_bass_kernel_spmd as _run

    nc = _bacc.Bacc("TRN2", target_bir_lowering=False, num_devices=1)
    arrays, ins, outs = {}, {}, {}
    for name in _INS:
        a = np.ascontiguousarray(inputs[name])
        arrays[f"in_{name}"] = a
        ins[name] = nc.dram_tensor(f"in_{name}", a.shape, F32, kind="ExternalInput").ap()
    arrays["in_consts"] = constants()
    ins["consts"] = nc.dram_tensor("in_consts", (P, NCONST), F32, kind="ExternalInput").ap()
    for name, shape in _OUTS:
        outs[name] = nc.dram_tensor(f"out_{name}", shape, F32, kind="ExternalOutput").ap()
    program(nc, ins, outs)
    r = _run(nc, [arrays], core_ids=[0])
    return tuple(r.results[0][f"out_{name}"] for name, _ in _OUTS)
```

```python
from contextlib import ExitStack

import numpy as np
import concourse.bass as bass
from concourse import mybir

F32 = mybir.dt.float32
F16 = mybir.dt.float16
I32 = mybir.dt.int32
U32 = mybir.dt.uint32
ALU = mybir.AluOpType
ACT = mybir.ActivationFunctionType
AX = mybir.AxisListType

P = 128
DEPTH = 2
D = 1024
KC = D // P
SEQ, DEC, PAST = 512, 64, 512
NT = 5
TOK = SEQ + DEC
HD = 64
ROT = 8
CW = 31
NE = 16
DE = 256
EPS = 1e-6
BIG = 1e30
MARK = -3e38
XJ = (2 * TOK - 1) // P
XROW = NE * P
IW_SCALE = float(np.float32(8 ** -0.5 * 64 ** -0.5))
CQ, CK, CV, CIQ, CIK, CIW, CU = 0, 512, 640, 768, 1280, 1344, 1352
K_ID, K_UT, K_ONE, K_IOTA, K_M0 = 0, 128, 256, 384, 512
K_COS, K_SIN, K_TOK, K_E16, K_ROW, NCONST = 640, 680, 720, 725, 741, 757


def constants():
    c = np.zeros((P, NCONST), np.float32)
    i = np.arange(P)
    c[:, K_ID:K_ID + P] = np.eye(P)
    c[:, K_UT:K_UT + P] = i[:, None] < i[None, :]
    c[:, K_ONE:K_ONE + P] = 1.0
    c[:, K_IOTA:K_IOTA + P] = i[None, :]
    c[:64, K_M0 + 64:K_M0 + P] = -BIG
    inv = np.float32(500000.0) ** (-np.arange(ROT, dtype=np.float32) / np.float32(ROT))
    pos = (np.arange(NT)[None, :] * P + i[:, None]).astype(np.float32)
    ang = pos[:, :, None] * inv[None, None, :].astype(np.float32)
    c[:, K_COS:K_COS + 40] = np.cos(ang).reshape(P, 40)
    c[:, K_SIN:K_SIN + 40] = np.sin(ang).reshape(P, 40)
    c[:, K_TOK:K_TOK + NT] = pos
    c[:, K_E16:K_E16 + NE] = np.arange(NE)[None, :]
    c[:, K_ROW:K_ROW + NE] = np.arange(NE)[None, :] * P
    return c


def rows_of(t):
    return P if t < 4 else DEC


PARTS = ((P, 0, 4), (DEC, 4, 5))
SCORED = (4, 3, 2, 1)
NKEYS = {0: 128, 1: 256, 2: 384, 3: 512, 4: 576}
TOPK = {1: 128, 2: 128, 3: 128, 4: 144}
MSK_AT = {1: 0, 2: 256, 3: 640, 4: 1152}
ATTN = (0, 4, 3, 2, 1)
NSMALL = 18
DVE_CONV = 3
NCDVE, NCPOOL = DVE_CONV * CW, (4 - DVE_CONV) * CW
S_SS, S_VAR, S_RS, S_M8, S_QS, S_MX, S_NMX, S_SUM, S_INV = 0, 5, 10, 16, 24, 124, 132, 140, 156
S_FS, S_FV, S_FR, S_AT = 164, 169, 174, 180
R_LG, R_GM, R_EQ, R_CAND, R_MI, R_GOH, R_GE, R_EM, R_M1 = 0, 100, 105, 125, 145, 150, 170, 190, 270
R_EQ1, R_MI1, R_OH1, R_M2, R_OH2, R_Z, R_W, R_G1, R_G2 = 275, 355, 360, 440, 445, 525, 530, 550, 555
R_PG, R_AS, R_POS, R_TMP, R_S = 560, 565, 645, 725, 805
R_PL, R_XC, R_RT, R_UP = 275, 16, 645, 816


def program(nc, A, O):
    ctx = ExitStack()
    with ctx:
        def sb(name, shape, dt=F32):
            return ctx.enter_context(nc.sbuf_tensor(name, shape, dt))

        def sem(name):
            return ctx.enter_context(nc.semaphore(name))

        def dram(name, shape):
            return nc.dram_tensor(name, shape, F32, kind="Internal").ap()

        W = sb("W", [P, 6, 2048])
        C = sb("C", [P, NCONST])
        X = sb("X", [P, NT, D])
        hT = sb("hT", [P, KC, TOK])
        gt = sb("gt", [P, 2, D])
        vrows = sb("vrows", [52, P])
        vT = sb("vT", [P, 52])
        crows = sb("crows", [62, 512])
        taps = sb("taps", [P, 4, CW])
        gq = sb("gq", [P, 2, HD])
        wr = sb("wr", [P, KC, 20])
        rb = sb("rb", [P, 20])
        ck = sb("ck", [P, 4, P])
        cv = sb("cv", [P, 4, P])
        cik = sb("cik", [P, 4, P])
        vrow = sb("vrow", [P, NT, P])
        iw = sb("iw", [P, NT, 8])
        small = sb("small", [P, 200])
        jobs = sb("jobs", [P, XJ + 1], I32)
        idx = sb("idx", [P, NE + 1], U32)
        zeros = sb("zeros", [P, 256])
        sid = sb("sid", [P, 2 * NT], U32)
        route = sb("route", [P, 896])
        tokf = sb("tokf", [P, NT], F16)
        ctmp = sb("ctmp", [P, 2, 606])
        arena = sb("arena", [P, 22320])

        def part(at, n, *shape):
            v = arena[:, at:at + n]
            if len(shape) == 2:
                return v.rearrange("p (a b) -> p a b", a=shape[0])
            if len(shape) == 3:
                return v.rearrange("p (a b c) -> p a b c", a=shape[0], b=shape[1])
            return v

        iqr = part(0, 3200, NT, 10, HD)
        qkr = part(3200, 3200, NT, 10, HD)
        iqf, qkf = part(0, 3200, NT, 640), part(3200, 3200, NT, 640)
        qT = part(6400, 2304, 4, TOK)
        kT = [part(8704, 1088), part(9792, 1088)]
        gT = part(10880, 2544, 4, 636)
        cy = part(17336, 2424, 4, 606)
        msk = part(13424, 1728)
        XN = part(15152, 5120, NT, D)
        rel = part(15152, 1728, 3, 576)
        sq = part(0, 3200, NT, 10, HD)
        PR = part(0, 4608, 8, 576)
        pT = part(19760, 2560, 5, 512)
        glu = part(19760, 2304, 4, 576)
        lnb = part(15152, 576)
        sqc = part(10880, 2304, 4, 576)
        wtmp = part(13424, 1024, 2, 512)
        AB = [part(17336, 2048, 2, D), part(10880, 2048, 2, D)]
        gf = part(15152, 1024)
        HR = part(5120, 2048, 2, D)
        oh = part(7168, 2048).bitcast(F16).rearrange("p (a e s) -> p a e s", a=2, e=NE)
        ohx = part(7168, 640).bitcast(F16).rearrange("p (a s) -> p a s", a=2 * NT)
        xg = part(9216, 2048, 2, D)
        xgT = part(11264, 2048, 2 * KC, P)
        sg = part(13312, 512, 2, DE)
        hid = part(13824, 512, 2, DE)
        hidT = part(14336, 512, 4, P)
        ys = part(14848, 2048, 2, D)
        yg = part(5120, 10240, 2 * NT, D)
        junk = part(21296, 1024)
        srows = part(0, 128)
        scT = part(128, 16, KC, 2)
        modr = part(256, DEPTH * 6 * D)

        ps = [ctx.enter_context(nc.psum_tensor(f"ps{i}", [P, 512], F32)) for i in range(8)]

        mod_d = dram("mod_d", [DEPTH, 2, 6, D])
        h_d = dram("h_d", [TOK, D])
        y_d = dram("y_d", [XROW + XJ * P, D])

        ident = C[:, K_ID:K_ID + P]
        ones = C[:, K_ONE:K_ONE + P]

        w_ld = [sem(f"w_ld{i}") for i in range(6)]
        w_free = [sem(f"w_free{i}") for i in range(6)]
        s_c, s_x, s_r = sem("s_c"), sem("s_x"), sem("s_r")
        s_silu, s_cT, s_cTc, s_ada, s_adae = (sem(n) for n in ("s_silu", "s_cT", "s_cTc", "s_ada", "s_adae"))
        s_b, s_mst = sem("s_b"), sem("s_mst")
        s_init = sem("s_init")
        s_xg = [sem(f"s_xg{i}") for i in range(2)]
        s_yg = [sem(f"s_yg{i}") for i in range(NT)]
        s_xx = sem("s_xx")
        n_cnt = sem("n_cnt")
        y_out = sem("y_out")
        s_sum = sem("s_sum")
        s_fin = sem("s_fin")
        sp_steps = sem("sp_steps")
        go = {n: sem(f"go_{n}") for n in ("pe", "act", "pool")}
        arrived = sem("arrived")
        names = ("small_ld", "gt_ld", "gtf_ld", "ab_ld", "vecT", "vecC", "var", "root", "xn", "nT", "nTa", "nTd",
                 "proj", "proja", "ropei", "dch", "pch", "tr", "tra", "dots", "rel", "score", "sqd", "qvar", "qroot",
                 "qinv", "ropeq", "ropes", "uproj", "glua", "glup", "cdve", "cpool", "lgt", "ttr", "nmx", "pexp", "inv", "pn", "pt",
                 "pta", "pv", "on", "lnm", "lnx", "lnsq", "lnv", "lnr", "lny", "mixy", "wo", "wod", "xadd",
                 "fsum", "fvar", "froot", "hrow", "hst0", "hst1", "hTt", "hTa", "rl", "gdiff", "gexp", "zdiff", "zexp",
                 "assign", "pos", "ready", "cst", "csta", "outst", "comb", "yg1", "ygt", "zst",
                 "oh", "ohu", "idx", "tx", "txa", "txd", "gu", "sg", "hid", "ht", "hta", "dn", "ya", "yd", "yst0", "yst1")
        L = {n: sem("l_" + n) for n in names}
        names = ("oh", "idx", "idc", "tx", "txa", "txd", "gu", "sg", "hid", "ht", "hta", "dn", "ya", "yd", "yst", "rch")
        M = {n: sem("x_" + n) for n in names}
        lrange = range(min(s.num for s in L.values()), max(s.num for s in L.values()) + 1)
        mrange = range(min(s.num for s in M.values()), max(s.num for s in M.values()) + 1)
        assert len(lrange) == len(L) and len(mrange) == len(M)

        block = ctx.enter_context(nc.Block())

        def leave(eng, name):
            eng.drain().then_inc(arrived, 1)
            eng.wait_ge(go[name], 1)
            eng.sem_clear(go[name])

        def release(dve, sems):
            dve.drain()
            dve.wait_ge(arrived, 3)
            dve.sem_clear(arrived)
            dve.sem_clear(sems)
            for g in go.values():
                dve.sem_inc(g, 1)

        def keys_of(t):
            return (0, NKEYS[t]) if t < 4 else (512, 1024)

        def chunks_of(t):
            return [(c, P) for c in range(t + 1 if t < 4 else 4)] + ([(4, DEC)] if t == 4 else [])

        GROUPS = [(t, g) for t in ATTN for g in range(2)]
        PT0 = [sum(len(chunks_of(t)) for t, _ in GROUPS[:n]) for n in range(11)]

        def logit_bank(job):
            return job % 3 if job < 8 else job % 2 if job < 16 else (job + 2) % 3

        def rope(eng, E, rows, r, t0, t1, at, s_chain, n_chain, done, count):
            nt = t1 - t0
            shape = [r, nt, 10, ROT]

            def angle(k):
                return C[0:r, k + ROT * t0:k + ROT * t1].rearrange("p (t d) -> p t d", d=ROT).unsqueeze(2).to_broadcast(shape)
            x1, x2 = rows[0:r, t0:t1, :, 0:ROT], rows[0:r, t0:t1, :, ROT:2 * ROT]
            tmp = [arena[0:r, at + 400 * j:at + 400 * j + nt * 10 * ROT].rearrange("p (t h d) -> p t h d", t=nt, h=10) for j in range(4)]
            for j, (x, k) in enumerate(((x1, K_COS), (x2, K_SIN), (x2, K_COS), (x1, K_SIN))):
                n_chain[0] += 1
                E.tensor_tensor(tmp[j], x, angle(k), ALU.mult).then_inc(s_chain, 1)
            eng.wait_ge(s_chain, n_chain[0])
            n_chain[0] += 1
            E.tensor_tensor(x1, tmp[0], tmp[1], ALU.subtract).then_inc(s_chain, 1)
            E.tensor_tensor(x2, tmp[2], tmp[3], ALU.add).then_inc(done, 1)
            eng.wait_ge(s_chain, n_chain[0])
            eng.wait_ge(done, count)

        def norm_qk(E, chain, r, t0, t1):
            inv = small[0:r, S_QS + 50 + 10 * t0:S_QS + 50 + 10 * t1].rearrange("p (t h) -> p t h", h=10)
            v = qkr[0:r, t0:t1]
            chain(E.tensor_tensor(v, v, inv.unsqueeze(3).to_broadcast([r, t1 - t0, 10, HD]), ALU.mult))
            for a, b, j in ((0, 8, 0), (8, 10, 1)):
                v = qkr[0:r, t0:t1, a:b, :]
                chain(E.tensor_tensor(v, v, gq[0:r, j, :].unsqueeze(1).unsqueeze(1).to_broadcast([r, t1 - t0, b - a, HD]), ALU.mult))

        @block.sync
        def _(sp):
            n0 = sp.alloc_register("sp_uses_012")
            n3 = sp.alloc_register("sp_uses_3")
            n4 = sp.alloc_register("sp_uses_45")
            further = sp.alloc_register("sp_further")
            expert = sp.alloc_register("sp_expert")

            def wait(s, value):
                sp.wait_ge(s, value)
                sp.sem_inc(sp_steps, 1)

            def load(slot, use, src):
                if not (isinstance(use, int) and use == 0):
                    wait(w_free[slot], use)
                n = src.shape[-1] * src.shape[-2]
                dst = W[:, slot, :]
                dst = dst[:, 0:n].rearrange("p (k c) -> p k c", c=src.shape[-1])
                sp.dma_start(dst, src).then_inc(w_ld[slot], 16)

            wada = A["w_ada"].rearrange("l (k p) c -> l p k c", p=P)
            win = A["w_in"].rearrange("l (k p) c -> l p k c", p=P)
            wout = A["w_out"].rearrange("l (k p) c -> l p k c", p=P)
            wexp = [A[n].rearrange("l e (k p) f -> l e p k f", p=P) for n in ("w_gate", "w_up", "w_down")]

            def ada(l, third, first=False):
                for c in range(3):
                    for hf in range(2):
                        src = wada[l, :, 4 * hf:4 * hf + 4, bass.ds(third * 1536 + c * 512, 512)]
                        load(2 * c + hf, 0 if first else third + 4 * l, src)

            ada(0, 0, True)
            with sp.Fori(1, 4) as third:
                ada(0, third)
            with sp.Fori(0, 4) as third:
                ada(1, third)
            sp.reg_mov(n0, 8)
            sp.reg_mov(n3, 8)
            sp.reg_mov(n4, 8)

            with sp.Fori(0, DEPTH) as l:
                b0, b3, b4 = sp.snap(n0), sp.snap(n3), sp.snap(n4)
                base = [b0, b0, b0, b3, b4, b4]
                for c in range(8):
                    for hf in range(2):
                        s = 2 * (c % 3) + hf
                        ks = slice(4 * hf, 4 * hf + 4)

                        def cols(w, c0, c1):
                            return w[bass.ds(l, 1), :, ks, c0:c1].rearrange("l p k c -> (l p) k c")
                        if c in (0, 1):
                            c0 = CU + 512 * hf + 256 * c
                            src = win[bass.ds(l, 1), :, :, c0:c0 + 256].rearrange("l p k c -> (l p) k c")
                        else:
                            src = {2: lambda: cols(win, CIQ, CIK), 3: lambda: cols(win, CIK, CU), 4: lambda: cols(win, CK, CIQ),
                                   5: lambda: cols(win, CQ, CK), 6: lambda: cols(wout, 0, 512),
                                   7: lambda: cols(wout, 512, 1024)}[c]()
                        load(s, base[s] + c // 3, src)
                with sp.Fori(0, NE // 2) as i:
                    for u in range(2):
                        for j, w in enumerate(wexp):
                            s = 3 * u + j
                            src = w[bass.ds(l, 1), bass.ds(i * 2 + u, 1)].rearrange("l e p k f -> (l e p) k f")
                            load(s, base[s] + (3 if s < 4 else 2) + i, src)
                sp.reg_add(n0, n0, 11)
                sp.reg_add(n3, n3, 11)
                sp.reg_add(n4, n4, 10)
                wait(n_cnt, l + 1)
                sp.reg_load(further, jobs[0:1, XJ:XJ + 1])
                with sp.If_ne(further, 0):
                    with sp.Fori(0, sp.snap(further, min_val=0, max_val=XJ)) as x:
                        sp.reg_load(expert, jobs[0:1, bass.ds(x, 1)])
                        e = sp.snap(expert, min_val=0, max_val=NE - 1)
                        for s, w in enumerate(wexp):
                            load(s, sp.snap(n0), w[bass.ds(l, 1), bass.ds(e, 1)].rearrange("l e p k f -> (l e p) k f"))
                        sp.reg_add(n0, n0, 1)
            sp.wait_ge(s_x, 32)

        @block.tensor
        def _(pe):
            T = nc.tensor
            n0 = pe.alloc_register("pe_uses_012")
            n3 = pe.alloc_register("pe_uses_3")
            n4 = pe.alloc_register("pe_uses_45")
            further = pe.alloc_register("pe_further")
            gathers = pe.alloc_register("pe_gathers")
            pe.reg_mov(gathers, 0)
            done_units = []

            def count(ins, done):
                if done is not None:
                    ins.then_inc(done, 1)
                elif done_units:
                    ins.then_inc(w_free[done_units.pop(0)], 1)

            def products(out, pairs, done=None, before=None, halfway=None):
                for n, (l, r) in enumerate(pairs):
                    if before is not None and n == len(pairs) // 2:
                        before()
                    ins = T.matmul(out, l, r, start=n == 0, stop=n == len(pairs) - 1, skip_group_check=True)
                    if halfway is not None and n == len(pairs) // 2:
                        assert not done_units
                        done_units.append(halfway)
                    count(ins, done if n == len(pairs) - 1 else None)

            def turn(outs_ins, done):
                for n, (o, i) in enumerate(outs_ins):
                    m = i.shape[0]
                    count(T.transpose(o, i, ident[0:m, 0:m]), done if n == len(outs_ins) - 1 else None)

            pe.wait_ge(s_c, 16)
            pe.wait_ge(s_silu, 1)
            turn([(ps[7][:, 0:16], srows[0:16, :])], s_cT)
            pe.wait_ge(s_cTc, 1)
            with pe.Fori(0, DEPTH) as l:
                with pe.Fori(0, 2) as h:
                    for u in range(2):
                        g = l * 4 + h * 2 + u
                        for c in range(3):
                            pe.wait_ge(w_ld[2 * c], (g + 1) * 16)
                            pe.wait_ge(w_ld[2 * c + 1], (g + 1) * 16)
                            if c == 0:
                                pe.wait_ge(s_adae, g + 1)
                            wv = [W[:, 2 * c + q, :].rearrange("p (k c) -> p k c", c=512) for q in range(2)]
                            products(ps[3 * u + c][0:2, :], [(scT[:, k, :], wv[k // 4][:, k % 4, :]) for k in range(KC)],
                                     s_ada if c == 2 else None)
                            if c < 2:
                                done_units += [2 * c, 2 * c + 1]
                        for q in range(2):
                            T.transpose(ps[6][:, 0:128], ident, ident).then_inc(w_free[4 + q], 1)
            pe.reg_mov(n0, 8)
            pe.reg_mov(n3, 8)
            pe.reg_mov(n4, 8)
            with pe.Fori(0, DEPTH) as l:
                b0, b3, b4 = pe.snap(n0), pe.snap(n3), pe.snap(n4)
                base = [b0, b0, b0, b3, b4, b4]

                def came(s, use):
                    pe.wait_ge(w_ld[s], (base[s] + use + 1) * 16)

                pe.wait_ge(L["small_ld"], 16 * NSMALL)
                turn([(ps[6][:, 0:52], vrows[0:52, :])], L["vecT"])
                turn([(ps[7][:, 61 * c:61 * c + 61], crows[0:61, c * P:(c + 1) * P]) for c in range(4)], L["vecT"])
                pe.wait_ge(L["xn"], NT)
                for k in range(KC):
                    if k == 6:
                        pe.wait_ge(L["vecC"], 4)
                    turn([(ps[k][:, t * P:(t + 1) * P], XN[:, t, k * P:(k + 1) * P]) for t in range(4)], L["nT"])
                for q, s_read in ((0, "nTa"), (1, "nTd")):
                    pe.wait_ge(L[s_read], 1)
                    turn([(ps[q][:, k * DEC:(k + 1) * DEC], XN[0:DEC, 4, k * P:(k + 1) * P]) for k in range(q, KC, 2)], L["nT"])
                pe.wait_ge(L["nTa"], 8)
                pe.wait_ge(L["nTd"], 8)

                def tokens(t):
                    return slice(t * P, t * P + rows_of(t))

                def project(c, n, job, ring, evac, done):
                    s = 2 * (c % 3)
                    wv = [W[:, s + q, 0:4 * n].rearrange("p (k c) -> p k c", c=n) for q in range(2)]
                    for t in range(NT):
                        if job + t == 2 and c == 2:
                            pe.wait_ge(L["glua"], 4)
                        if job + t >= len(ring):
                            pe.wait_ge(evac, job + t - len(ring) + 1)
                        if t == 0:
                            came(s, c // 3)
                        products(ps[ring[(job + t) % len(ring)]][0:rows_of(t), 0:n],
                                 [(hT[:, k, tokens(t)], wv[k // 4][:, k % 4, :]) for k in range(KC)], done,
                                 before=(lambda: came(s + 1, c // 3)) if t == 0 else None,
                                 halfway=s if t == NT - 1 else None)
                    done_units.append(s + 1)

                for i in range(4):
                    c = i // 2
                    s = 2 * (c % 3)
                    if i >= 2:
                        pe.wait_ge(L["glua"], i - 1)
                    for n, (ab, smp) in enumerate(((0, 0), (1, 0), (0, 1), (1, 1))):
                        out = ps[7 if i % 2 == 0 else 2][:, ab * DEC:(ab + 1) * DEC] if smp else ps[3 + 2 * (i % 2) + ab][:, 0:SEQ]
                        tk = slice(SEQ, TOK) if smp else slice(0, SEQ)
                        if i % 2 == 0 and not smp:
                            came(s + ab, c // 3)
                        wv = W[:, s + ab, :].rearrange("p (k c) -> p k c", c=256)
                        products(out, [(wv[:, k, (i % 2) * P:(i % 2) * P + P], hT[:, k, tk]) for k in range(KC)], L["uproj"])
                        if i % 2 == 1 and smp:
                            done_units.append(s + ab)
                for n, (c, w) in enumerate(((2, 512), (3, 72))):
                    project(c, w, 5 * n, (0, 1, 2), L["proja"], L["proj"])
                    if n == 1:
                        pe.wait_ge(L["glup"], 4)
                        turn([(ps[6][0:30, c * P:(c + 1) * P], gT[:, c, 512:542]) for c in range(4)], L["cst"])
                        turn([(ps[7][0:30, c * P:(c + 1) * P], gT[:, c, 606:636]) for c in range(4)], L["cst"])

                def turn_qk(src, past, job):
                    for i in range(5):
                        turn([(ps[3 + i][:, t * P:(t + 1) * P], src[:, t, i * P:(i + 1) * P]) for t in range(4)], L["tr"])
                    pe.wait_ge(L["tra"], job + 1)
                    turn([(ps[3][:, i * DEC:(i + 1) * DEC], src[0:DEC, 4, i * P:(i + 1) * P]) for i in range(5)], L["tr"])
                    pe.wait_ge(L["tra"], job + 2)
                    turn([(ps[4][:, c * P:(c + 1) * P], past[:, c]) for c in range(4)], L["tr"])
                pe.wait_ge(L["ropei"], 2)
                pe.wait_ge(L["csta"], 2)
                turn_qk(iqf, cik, 0)
                pe.wait_ge(L["tra"], 7)
                for n, (t, h) in enumerate((t, h) for t in SCORED for h in range(8)):
                    if n >= 3:
                        pe.wait_ge(L["rel"], n - 2)
                    hp = slice(64 * (h % 2), 64 * (h % 2) + 64)
                    a, b = keys_of(t)
                    q = qT[hp, h // 2, tokens(t)]
                    if t == 4:
                        if n >= 2:
                            pe.wait_ge(L["rel"], n - 1)
                        count(T.matmul(ps[3 + n % 2][0:DEC, 0:DEC], q, kT[0][hp, 1024:1088], start=True, stop=True), None)
                    count(T.matmul(ps[5 + n % 3][0:rows_of(t), 0:b - a], q, kT[0][hp, a:b], start=True, stop=True), L["dots"])
                project(4, 256, 10, (0, 1, 2), L["proja"], L["proj"])
                project(5, 512, 15, (0, 1, 2), L["proja"], L["proj"])
                pe.wait_ge(L["rel"], 32)
                pe.wait_ge(L["cdve"], NCDVE)
                pe.wait_ge(L["cpool"], NCPOOL)
                products(ps[3][:, 0:SEQ], [(ones, cy[:, c, 0:SEQ]) for c in range(4)], L["lnm"])
                products(ps[4][:, 0:DEC], [(ones, cy[:, c, 542:606]) for c in range(4)], L["lnm"])
                pe.wait_ge(L["lnsq"], 2)
                products(ps[5][:, 0:SEQ], [(ones, sqc[:, c, 0:SEQ]) for c in range(4)], L["lnv"])
                products(ps[6][:, 0:DEC], [(ones, sqc[:, c, SEQ:TOK]) for c in range(4)], L["lnv"])
                pe.wait_ge(L["ropeq"], 1)
                pe.wait_ge(L["ropes"], 1)
                pe.wait_ge(L["lnr"], 1)
                turn_qk(qkf, ck, 7)
                pe.wait_ge(L["tra"], 14)

                def logits(n):
                    t, g = GROUPS[n]
                    a, b = keys_of(t)
                    hp = slice(64 * g, 64 * g + 64)
                    for i in range(4):
                        job = 4 * n + i
                        if job >= 3:
                            pe.wait_ge(L["ttr"], job - 1 if 2 <= n <= 4 else job - 2)
                        q = qT[hp, i, tokens(t)]
                        if t == 4:
                            T.matmul(ps[2 + job % 2][0:DEC, 0:DEC], q, kT[1][hp, 1024:1088], start=True, stop=True)
                        T.matmul(ps[logit_bank(job)][0:rows_of(t), 0:b - a], q, kT[1][hp, a:b], start=True, stop=True).then_inc(L["lgt"], 1)

                tj = [0]

                def bank_for_turn():
                    j = tj[0]
                    if j >= 2:
                        pe.wait_ge(L["pta"], j - 1)
                    tj[0] += 1
                    return ps[4 + j % 2]

                logits(0)
                logits(1)
                for n, (t, g) in enumerate(GROUPS):
                    m = rows_of(t)
                    pe.wait_ge(L["pn"], n + 1)
                    assert tj[0] == PT0[n]
                    for c, kn in chunks_of(t):
                        o = bank_for_turn()
                        turn([(o[0:kn, i * m:(i + 1) * m], PR[0:m, 4 * (n % 2) + i, c * P:c * P + kn]) for i in range(4)], L["pt"])
                    if n + 2 < len(GROUPS):
                        logits(n + 2)
                    if n >= 2:
                        pe.wait_ge(L["on"], n - 1)
                    last = chunks_of(t)[-1][0]
                    pe.wait_ge(L["pta"], PT0[n] + len(chunks_of(t)))
                    for c, kn in chunks_of(t):
                        v = (vrow[0:kn, c, :] if t < 4 else cv[:, c, :] if c < 4 else vrow[0:kn, 4, :])[:, g * 64:g * 64 + 64]
                        heads = pT[0:kn, c, 0:4 * m].rearrange("p (j a t) -> p j a t", j=2, a=2)
                        for a in range(2):
                            ins = T.matmul(ps[6 + n % 2][64 * a:64 * a + 64, 0:2 * m], v, heads[:, :, a, :],
                                           start=c == 0, stop=c == last, skip_group_check=True)
                    ins.then_inc(L["pv"], 1)
                pe.wait_ge(L["mixy"], 8)
                pe.wait_ge(L["on"], 10)
                def turn_h(t):
                    m = rows_of(t)
                    pe.wait_ge(L["hrow"], t + 1)
                    if t >= 2:
                        pe.wait_ge(L["hTa"], 2 * (t - 1))
                    for q in range(2):
                        turn([(ps[2 * (t % 2) + q][:, j * m:(j + 1) * m], HR[0:m, t % 2, (4 * q + j) * P:(4 * q + j + 1) * P])
                              for j in range(4)], L["hTt"])

                def route_tile(t):
                    pe.wait_ge(L["hTa"], 2 * (t + 1))
                    products(ps[4][0:rows_of(t), t * 20:t * 20 + 20], [(hT[:, k, tokens(t)], wr[:, k, :]) for k in range(KC)], L["rl"])

                for t in range(NT):
                    for hf in range(2):
                        n = 2 * t + hf
                        if n >= 3:
                            pe.wait_ge(L["wod"], n - 2)
                        for q in range(2):
                            if t == 0:
                                came(2 * hf + q, 2)
                            wv = W[:, 2 * hf + q, :].rearrange("p (k c) -> p k c", c=512)
                            for k in range(4):
                                last = q == 1 and k == 3
                                ins = T.matmul(ps[5 + n % 3][0:rows_of(t), :], hT[:, 4 * q + k, tokens(t)], wv[:, k, :],
                                               start=q == 0 and k == 0, stop=last, skip_group_check=True)
                                count(ins, L["wo"] if last else None)
                            if t == NT - 1:
                                done_units.append(2 * hf + q)
                        if t >= 1 and hf == 0:
                            turn_h(t - 1)
                    if t >= 1:
                        route_tile(t - 1)
                turn_h(NT - 1)
                route_tile(NT - 1)
                assert not done_units
                pe.wait_ge(L["assign"], 1)
                sel = route[:, R_AS:R_AS + 80]
                T.matmul(ps[5][:, 0:80], C[:, K_UT:K_UT + P], sel, start=True, stop=True)
                T.matmul(ps[5][:, 80:160], ones, sel, start=True, stop=True).then_inc(L["pos"], 1)
                for t in range(NT):
                    pe.wait_ge(L["oh"], t + 1)
                    for e in range(NE):
                        ins = T.matmul(ps[6][:, e:e + 1], oh[:, t % 2, e, :], tokf[:, t:t + 1], start=t == 0 and e == 0,
                                       stop=t == NT - 1, skip_group_check=True)
                    ins.then_inc(L["ohu"], 1)

                def uses(s):
                    return 3 if s < 4 else 2

                def step(i, u, head, tail):
                    e = i * 2 + u
                    s = 3 * u
                    pe.wait_ge(L["txa"], e + 1)
                    pe.wait_ge(L["txd"], e + 1)
                    came(s, uses(s) + i)
                    if not (head and u == 0):
                        pe.wait_ge(L["hid"], e)
                    gv = W[:, s, :].rearrange("p (k f) -> p k f", f=DE)
                    uv = W[:, s + 1, :].rearrange("p (k f) -> p k f", f=DE)
                    products(ps[2][:, 0:DE], [(xgT[:, u * KC + k, :], gv[:, k, :]) for k in range(KC)])
                    done_units.append(s)
                    came(s + 1, uses(s + 1) + i)
                    products(ps[2][:, DE:2 * DE], [(xgT[:, u * KC + k, :], uv[:, k, :]) for k in range(KC)], L["gu"])
                    done_units.append(s + 1)
                    if not (tail and u == 1):
                        un = 1 - u
                        pe.wait_ge(s_xg[un], (l * (NE // 2) + i + 1 + u) * 16)
                        for q in range(2):
                            turn([(ps[q][:, j * P:(j + 1) * P], xg[:, un, (4 * q + j) * P:(4 * q + j + 1) * P])
                                  for j in range(4)], L["tx"])
                    if not (head and u == 0):
                        down(i, u, e - 1, 1 - u, i - 1 + u, head and u == 1)
                    pe.wait_ge(L["hid"], e + 1)
                    turn([(ps[5][:, j * P:(j + 1) * P], hid[:, u, j * P:(j + 1) * P]) for j in range(2)], L["ht"])

                def down(i, u, e, par, use, first):
                    s = 3 * par + 2
                    pe.wait_ge(L["hta"], e + 1)
                    came(s, uses(s) + use)
                    dv = W[:, s, :].rearrange("p (k f) -> p k f", f=D)
                    for q in range(2):
                        if not first:
                            pe.wait_ge(L["ya" if q == 0 else "yd"], e)
                        products(ps[3 + q][:, :], [(hidT[:, 2 * par + k, :], dv[:, k, q * 512:(q + 1) * 512]) for k in range(2)],
                                 L["dn"])
                    done_units.append(s)

                pe.wait_ge(s_xg[0], l * (NE * 8) + 16)
                for q in range(2):
                    turn([(ps[q][:, j * P:(j + 1) * P], xg[:, 0, (4 * q + j) * P:(4 * q + j + 1) * P]) for j in range(4)], L["tx"])
                for u in range(2):
                    step(0, u, True, False)
                with pe.Fori(1, NE // 2 - 1) as i:
                    for u in range(2):
                        step(i, u, False, False)
                for u in range(2):
                    step(NE // 2 - 1, u, False, True)
                down(None, None, NE - 1, 1, NE // 2 - 1, False)

                while done_units:
                    T.transpose(ps[7][:, 0:128], ident, ident).then_inc(w_free[done_units.pop(0)], 1)
                pe.reg_add(n0, n0, 11)
                pe.reg_add(n3, n3, 11)
                pe.reg_add(n4, n4, 10)
                pe.wait_ge(L["ready"], 1)
                pe.reg_load(further, jobs[0:1, XJ:XJ + 1])
                with pe.If_ne(further, 0):
                    pe.wait_ge(L["ya"], NE)
                    pe.wait_ge(L["yd"], NE)
                    with pe.Fori(0, pe.snap(further, min_val=0, max_val=XJ)):
                        use = pe.snap(n0)
                        pe.wait_ge(M["oh"], 1)
                        products(ps[6][:, 0:1], [(ohx[:, k * NT + t, :], tokf[:, t:t + 1]) for k in range(2) for t in range(NT)], M["idx"])
                        pe.wait_ge(s_xx, pe.snap(gathers) * 16 + 16)
                        for q in range(2):
                            turn([(ps[q][:, j * P:(j + 1) * P], xg[:, 0, (4 * q + j) * P:(4 * q + j + 1) * P]) for j in range(4)], M["tx"])
                        pe.wait_ge(M["txa"], 1)
                        pe.wait_ge(M["txd"], 1)
                        for s in range(2):
                            pe.wait_ge(w_ld[s], use * 16 + 16)
                            wv = W[:, s, :].rearrange("p (k f) -> p k f", f=DE)
                            products(ps[2][:, s * DE:(s + 1) * DE], [(xgT[:, k, :], wv[:, k, :]) for k in range(KC)], M["gu"])
                        pe.wait_ge(M["hid"], 1)
                        turn([(ps[5][:, j * P:(j + 1) * P], hid[:, 0, j * P:(j + 1) * P]) for j in range(2)], M["ht"])
                        pe.wait_ge(M["hta"], 1)
                        pe.wait_ge(w_ld[2], use * 16 + 16)
                        dv = W[:, 2, :].rearrange("p (k f) -> p k f", f=D)
                        for q in range(2):
                            products(ps[3 + q][:, :], [(hidT[:, k, :], dv[:, k, q * 512:(q + 1) * 512]) for k in range(2)], M["dn"])
                        for s in range(3):
                            T.transpose(ps[7][:, 0:128], ident, ident).then_inc(w_free[s], 1)
                        pe.reg_add(n0, n0, 1)
                        pe.reg_add(gathers, gathers, 1)
                        leave(pe, "pe")
                leave(pe, "pe")

        @block.scalar
        def _(act):
            S = nc.scalar
            further = act.alloc_register("act_further")
            act.dma_start(C[:, :], A["consts"]).then_inc(s_c, 16)
            act.dma_start(srows[0:8, :], A["c_prompt"].rearrange("b (k p) -> (b k) p", p=P)).then_inc(s_r, 16)
            act.dma_start(srows[8:16, :], A["c_sample"].rearrange("b (k p) -> (b k) p", p=P)).then_inc(s_r, 16)
            act.dma_start(modr[0:2, :], A["b_ada"].rearrange("(o l) k -> o (l k)", o=1).broadcast_to([2, DEPTH * 6 * D])).then_inc(s_b, 16)
            act.dma_start(X[:, 0:4, :], A["x_prompt"].rearrange("b (t p) d -> p (b t) d", p=P)).then_inc(s_x, 16)
            act.dma_start(X[0:DEC, 4, :], A["x_sample"][0]).then_inc(s_x, 16)
            act.wait_ge(s_r, 32)
            S.activation(srows[0:16, :], srows[0:16, :], ACT.Silu).then_inc(s_silu, 1)
            act.wait_ge(s_x, 32)
            def sum_of_squares(t, before):
                m = rows_of(t)
                if not (isinstance(before, int) and before == 0):
                    act.wait_ge(s_sum, before)
                S.activation(junk[0:m], X[0:m, t, :], ACT.Square, accum_out=small[0:m, S_SS + t:S_SS + t + 1]).then_inc(s_sum, 1)

            act.wait_ge(s_init, 3)
            for t in range(NT):
                sum_of_squares(t, t)
            act.wait_ge(s_adae, 10)
            act.dma_start(mod_d.rearrange("l s q k -> s l (q k)"), modr[0:2, :].rearrange("s (l k) -> s l k", l=DEPTH)).then_inc(s_mst, 16)
            act.wait_ge(s_mst, 16)

            with act.Fori(0, DEPTH) as l:
                def at(name):
                    w = A[name][bass.ds(l, 1)]
                    return w

                act.wait_ge(L["var"], 1)
                S.activation(small[:, S_RS:S_RS + 5], small[:, S_VAR:S_VAR + 5], ACT.Sqrt).then_inc(L["root"], 1)

                ld = L["small_ld"]
                md = mod_d[bass.ds(l, 1)].rearrange("l s q (k p) -> s (l q k) p", p=P)
                act.dma_start(vrows[0:16, :], md[0, 0:16]).then_inc(ld, 16)
                act.dma_start(vrows[16:32, :], md[1, 0:16]).then_inc(ld, 16)
                act.dma_start(vrows[32:40, :], at("g_norm_mix").rearrange("l (k p) -> (l k) p", p=P)).then_inc(ld, 16)
                for n, name in enumerate(("conv_b", "ln_conv_g", "ln_conv_b")):
                    act.dma_start(vrows[40 + 4 * n:44 + 4 * n, :], at(name).rearrange("l (k p) -> (l k) p", p=P)).then_inc(ld, 16)
                act.dma_start(crows[0:31, :], at("conv_w").rearrange("l w c -> (l w) c")).then_inc(ld, 16)
                act.dma_start(crows[31:61, :], at("state_conv").rearrange("l b w c -> (l b w) c")).then_inc(ld, 16)
                act.dma_start(gq[:, 0, :], at("q_norm_g").broadcast_to([P, HD])).then_inc(ld, 16)
                act.dma_start(gq[:, 1, :], at("k_norm_g").broadcast_to([P, HD])).then_inc(ld, 16)
                act.dma_start(ck[:, :, :], at("cache_k").rearrange("l b (t p) n d -> p (l b t) (n d)", p=P)).then_inc(ld, 16)
                act.dma_start(cv[:, :, :], at("cache_v").rearrange("l b (t p) n d -> p (l b t) (n d)", p=P)).then_inc(ld, 16)
                for q in range(2):
                    act.dma_start(cik[:, :, 64 * q:64 * q + 64], at("cache_idx_k").rearrange("l b (t p) d -> p (l b t) d", p=P)).then_inc(ld, 16)
                act.dma_start(wr[:, :, 0:4], at("w_router_group").rearrange("l (k p) e -> p (l k) e", p=P)).then_inc(ld, 16)
                act.dma_start(wr[:, :, 4:20], at("w_router_expert").rearrange("l (k p) e -> p (l k) e", p=P)).then_inc(ld, 16)
                act.dma_start(rb[:, 0:4], at("b_router_group").broadcast_to([P, 4])).then_inc(ld, 16)
                act.dma_start(rb[:, 4:20], at("b_router_expert").broadcast_to([P, 16])).then_inc(ld, 16)
                mrows = mod_d[bass.ds(l, 1)].rearrange("l s q d -> s q l d")
                act.dma_start(gt[:, 0, :], mrows[0, 2].broadcast_to([P, D])).then_inc(L["gt_ld"], 16)
                act.dma_start(gt[0:DEC, 1, :], mrows[1, 2].broadcast_to([DEC, D])).then_inc(L["gt_ld"], 16)

                act.wait_ge(L["vecC"], 4)
                for k in range(0, KC, 2):
                    act.wait_ge(L["nT"], k + 1)
                    S.activation(hT[:, k, 0:SEQ], ps[k][:, :], ACT.Identity, bias=vT[:, k:k + 1],
                                 scale=small[:, S_AT + k:S_AT + k + 1]).then_inc(L["nTa"], 1)
                act.wait_ge(L["nT"], 9)
                for k in range(0, KC, 2):
                    S.activation(hT[:, k, SEQ:TOK], ps[0][:, k * DEC:(k + 1) * DEC], ACT.Identity, bias=vT[:, 16 + k:17 + k],
                                 scale=small[:, S_AT + 8 + k:S_AT + 9 + k]).then_inc(L["nTa"], 1)

                def out_of(job):
                    c, t = divmod(job, NT)
                    m = rows_of(t)
                    b = ps[job % 3]
                    act.wait_ge(L["proj"], job + 1)
                    if c == 0:
                        ins = S.copy(iqr[0:m, t, 0:8, :], b[0:m, :].rearrange("p (h d) -> p h d", d=HD))
                    elif c == 1:
                        for q in range(2):
                            S.copy(iqr[0:m, t, 8 + q, :], b[0:m, 0:HD])
                        ins = S.mul(iw[0:m, t, :], b[0:m, HD:HD + 8], IW_SCALE)
                    elif c == 2:
                        S.copy(qkf[0:m, t, 512:640], b[0:m, 0:P])
                        ins = S.copy(vrow[0:m, t, :], b[0:m, P:2 * P])
                    else:
                        ins = S.copy(qkr[0:m, t, 0:8, :].rearrange("p (i a) d -> p a i d", a=2),
                                     b[0:m, :].rearrange("p (a i d) -> p a i d", a=2, d=HD))
                    ins.then_inc(L["proja"], 1)
                def gates(i):
                    act.wait_ge(L["uproj"], 4 * i + 4)
                    if i >= 2:
                        act.wait_ge(L["glup"], i - 1)
                    for ab, f in ((0, ACT.Copy), (1, ACT.Sigmoid)):
                        S.activation(glu[:, 2 * (i % 2) + ab, 0:SEQ], ps[3 + 2 * (i % 2) + ab][:, :], f)
                        ins = S.activation(glu[:, 2 * (i % 2) + ab, SEQ:TOK], ps[7 if i % 2 == 0 else 2][:, ab * DEC:(ab + 1) * DEC], f)
                    ins.then_inc(L["glua"], 1)
                for i in range(4):
                    gates(i)
                for job in range(10):
                    out_of(job)
                for n in range(2):
                    act.wait_ge(L["cst"], n + 1)
                    S.copy(crows[32 * n:32 * n + 30, :], ps[6 + n][0:30, :]).then_inc(L["csta"], 1)
                act.wait_ge(L["csta"], 2)
                act.dma_start(O["new_conv_prompt"][bass.ds(l, 1)].rearrange("l b w c -> (l b w) c"), crows[0:30, :]).then_inc(L["outst"], 16)
                act.dma_start(O["new_conv_sample"][bass.ds(l, 1)].rearrange("l b w c -> (l b w) c"), crows[32:62, :]).then_inc(L["outst"], 16)

                def store(name, rows, src):
                    act.dma_start(rows(O[name][bass.ds(l, 1)]), src).then_inc(L["outst"], 16)

                def tiles(a):
                    return a.rearrange("l b (t p) n d -> p (l b t) (n d)", p=P)

                def row(a):
                    return a.rearrange("l b t n d -> (l b t) (n d)")
                act.wait_ge(L["ropei"], 2)
                store("new_idx_k_prompt", lambda a: a.rearrange("l b (t p) d -> p (l b t) d", p=P), iqf[:, 0:4, 512:576])
                store("new_idx_k_sample", lambda a: a.rearrange("l b t d -> (l b t) d"), iqf[0:DEC, 4, 512:576])

                def turned(job, keys):
                    for n in range(7):
                        act.wait_ge(L["tr"], job + n + 1)
                        b = ps[3 + n % 5]
                        if n < 4:
                            ins = S.copy(qT[:, n, 0:SEQ], b[:, :])
                        elif n == 4:
                            ins = S.copy(keys[:, 0:SEQ], b[:, :])
                        elif n == 5:
                            S.copy(qT[:, :, SEQ:TOK], b[:, 0:256].rearrange("p (i t) -> p i t", t=DEC))
                            ins = S.copy(keys[:, 1024:1088], b[:, 256:320])
                        else:
                            ins = S.copy(keys[:, SEQ:1024], b[:, :])
                        ins.then_inc(L["tra"], 1)
                act.wait_ge(s_init, 3)
                act.dma_start(y_d[XROW:XROW + XJ * P, :].rearrange("(p a) (b c) -> p (a b) c", p=P, c=256),
                              zeros[:, :].unsqueeze(1).to_broadcast([P, XJ * 4, 256])).then_inc(L["zst"], 16)
                turned(0, kT[0])
                for n, (t, h) in enumerate((t, h) for t in SCORED for h in range(8)):
                    m = rows_of(t)
                    a, b = keys_of(t)
                    act.wait_ge(L["dots"], n + 1)
                    if n >= 3:
                        act.wait_ge(L["score"], n - 2)
                    ins = S.activation(rel[0:m, n % 3, 0:b - a], ps[5 + n % 3][0:m, 0:b - a], ACT.Relu)
                    if t == 4:
                        ins = S.activation(rel[0:m, n % 3, 512:576], ps[3 + n % 2][0:m, 0:DEC], ACT.Relu)
                    ins.then_inc(L["rel"], 1)
                for job in range(10, 15):
                    out_of(job)
                act.wait_ge(L["proja"], 15)
                store("new_v_prompt", tiles, vrow[:, 0:4, :])
                store("new_v_sample", row, vrow[0:DEC, 4, :])
                for job in range(15, 20):
                    out_of(job)
                act.wait_ge(L["proja"], 20)
                act.wait_ge(L["outst"], 96)
                for t in range(NT):
                    m = rows_of(t)
                    S.activation(sq[0:m, t], qkr[0:m, t], ACT.Square).then_inc(L["sqd"], 1)
                act.wait_ge(L["qvar"], 1)
                S.activation(small[:, S_QS + 50:S_QS + 100], small[:, S_QS:S_QS + 50], ACT.Sqrt).then_inc(L["qroot"], 1)
                act.wait_ge(L["lnx"], 2)
                S.activation(sqc[:, :, 0:SEQ], cy[:, :, 0:SEQ], ACT.Square).then_inc(L["lnsq"], 1)
                S.activation(sqc[:, :, SEQ:TOK], cy[:, :, 542:606], ACT.Square).then_inc(L["lnsq"], 1)
                act.wait_ge(L["lnr"], 1)
                S.activation(lnb[:, :], lnb[:, :], ACT.Sqrt).then_inc(L["lnr"], 1)
                act.wait_ge(L["ropeq"], 1)
                act.wait_ge(L["ropes"], 1)
                store("new_k_prompt", tiles, qkf[:, 0:4, 512:640])
                store("new_k_sample", row, qkf[0:DEC, 4, 512:640])
                turned(7, kT[1])

                def exps(n):
                    t, g = GROUPS[n]
                    m = rows_of(t)
                    act.wait_ge(L["nmx"], n + 1)
                    for i in range(4):
                        r = PR[0:m, 4 * (n % 2) + i, 0:NKEYS[t]]
                        h = S_SUM + 8 * ((n // 2) % 2) + 4 * g + i
                        q = S_NMX + 4 * (n % 2) + i
                        ins = S.activation(r, r, ACT.Exp, bias=small[0:m, q:q + 1], accum_out=small[0:m, h:h + 1])
                    ins.then_inc(L["pexp"], 1)

                def outputs(n):
                    t, g = GROUPS[n]
                    m = rows_of(t)
                    act.wait_ge(L["pv"], n + 1)
                    S.copy(hT[:, 2 * g:2 * g + 2, t * P:t * P + m],
                           ps[6 + n % 2][:, 0:2 * m].rearrange("p (j t) -> p j t", j=2)).then_inc(L["on"], 1)

                exps(0)
                exps(1)
                act.wait_ge(L["lny"], 2)
                for c in range(4):
                    for d, a, n in ((0, 0, SEQ), (SEQ, 542, DEC)):
                        S.activation(hT[:, 4 + c, d:d + n], cy[:, c, a:a + n], ACT.Silu, bias=vT[:, 48 + c:49 + c],
                                     scale=vT[:, 44 + c:45 + c]).then_inc(L["mixy"], 1)
                for n, (t, g) in enumerate(GROUPS):
                    m = rows_of(t)
                    if n >= 1:
                        outputs(n - 1)
                    for q, (c, kn) in enumerate(chunks_of(t)):
                        job = PT0[n] + q
                        act.wait_ge(L["pt"], job + 1)
                        S.copy(pT[0:kn, c, 0:4 * m], ps[4 + job % 2][0:kn, 0:4 * m]).then_inc(L["pta"], 1)
                    if n + 2 < len(GROUPS):
                        if n >= 2:
                            act.wait_ge(L["inv"], n - 1)
                        exps(n + 2)
                    if n == 3:
                        act.wait_ge(L["mixy"], 8)
                        for b, q in enumerate((4, 3)):
                            act.dma_start(AB[0][:, b, :], mrows[0, q].broadcast_to([P, D])).then_inc(L["ab_ld"], 16)
                            act.dma_start(AB[1][0:DEC, b, :], mrows[1, q].broadcast_to([DEC, D])).then_inc(L["ab_ld"], 16)
                        act.dma_start(gf[:, :], A["g_norm_ffn"][bass.ds(l, 1)].broadcast_to([P, D])).then_inc(L["ab_ld"], 16)
                outputs(9)
                act.wait_ge(L["on"], 10)
                act.wait_ge(L["outst"], 16 * 8)

                for t in range(NT):
                    m = rows_of(t)
                    act.wait_ge(L["xadd"], 2 * t + 2)
                    if t >= 1:
                        act.wait_ge(L["fsum"], t)
                    S.activation(junk[0:m], X[0:m, t, :], ACT.Square, accum_out=small[0:m, S_FS + t:S_FS + t + 1]).then_inc(L["fsum"], 1)
                    act.wait_ge(L["fvar"], t + 1)
                    S.activation(small[:, S_FR + t:S_FR + t + 1], small[:, S_FV + t:S_FV + t + 1], ACT.Sqrt).then_inc(L["froot"], 1)
                    act.wait_ge(L["hrow"], t + 1)
                    act.dma_start(h_d[t * P:t * P + m, :], HR[0:m, t % 2, :]).then_inc(L[f"hst{t % 2}"], 16)
                    for q in range(2):
                        act.wait_ge(L["hTt"], 2 * t + q + 1)
                        S.copy(hT[:, 4 * q:4 * q + 4, t * P:t * P + m],
                               ps[2 * (t % 2) + q][:, 0:4 * m].rearrange("p (j t) -> p j t", j=4)).then_inc(L["hTa"], 1)
                act.dma_start(gt[:, 0, :], mrows[0, 5].broadcast_to([P, D])).then_inc(L["gtf_ld"], 16)
                act.dma_start(gt[0:DEC, 1, :], mrows[1, 5].broadcast_to([DEC, D])).then_inc(L["gtf_ld"], 16)
                act.wait_ge(L["gdiff"], 1)
                S.activation(route[:, R_GE:R_GE + 20], route[:, R_GE:R_GE + 20], ACT.Exp).then_inc(L["gexp"], 1)
                act.wait_ge(L["zdiff"], 1)
                S.activation(route[:, R_Z:R_Z + 5], route[:, R_Z:R_Z + 5], ACT.Exp).then_inc(L["zexp"], 1)

                act.wait_ge(L["ready"], 1)
                def turned_x(e, u):
                    act.wait_ge(L["tx"], e * 2 + 1)
                    S.copy(xgT[:, u * KC:u * KC + 4, :], ps[0][:, :].rearrange("p (j t) -> p j t", j=4)).then_inc(L["txa"], 1)

                def y_half(e, u):
                    act.wait_ge(L["dn"], e * 2 + 1)
                    S.copy(ys[:, u, 0:512], ps[3][:, :]).then_inc(L["ya"], 1)
                    act.wait_ge(L["yd"], e + 1)
                    act.wait_ge(L["ya"], e + 1)
                    act.dma_start(y_d[bass.ds(e * P, P), :], ys[:, u, :]).then_inc(L[f"yst{u}"], 16)

                def step(i, u, head, tail):
                    e = i * 2 + u
                    act.wait_ge(L["gu"], e + 1)
                    S.activation(sg[:, u, :], ps[2][:, 0:DE], ACT.Silu).then_inc(L["sg"], 1)
                    if not (tail and u == 1):
                        turned_x(e + 1, 1 - u)
                    if not (head and u == 0):
                        if not head and not (isinstance(i, int) and i - 1 + u == 0):
                            act.wait_ge(L[f"yst{1 - u}"], (i - 1 + u) * 16)
                        y_half(e - 1, 1 - u)
                    act.wait_ge(L["ht"], e + 1)
                    S.copy(hidT[:, 2 * u:2 * u + 2, :], ps[5][:, 0:256].rearrange("p (j t) -> p j t", j=2)).then_inc(L["hta"], 1)

                turned_x(0, 0)
                for u in range(2):
                    step(0, u, True, False)
                for u in range(2):
                    step(1, u, False, False)
                with act.Fori(2, NE // 2 - 1) as i:
                    for u in range(2):
                        step(i, u, False, False)
                for u in range(2):
                    step(NE // 2 - 1, u, False, True)
                act.wait_ge(L["yst1"], 16 * (NE // 2 - 1))
                y_half(NE - 1, 1)
                act.wait_ge(L["yst0"], 16 * (NE // 2))
                act.wait_ge(L["yst1"], 16 * (NE // 2))

                act.wait_ge(L["zst"], 16)
                act.reg_load(further, jobs[0:1, XJ:XJ + 1])
                with act.If_ne(further, 0):
                    with act.Fori(0, act.snap(further, min_val=0, max_val=XJ)) as x:
                        act.wait_ge(M["tx"], 1)
                        S.copy(xgT[:, 0:4, :], ps[0][:, :].rearrange("p (j t) -> p j t", j=4)).then_inc(M["txa"], 1)
                        act.wait_ge(M["gu"], 2)
                        S.activation(sg[:, 0, :], ps[2][:, 0:DE], ACT.Silu).then_inc(M["sg"], 1)
                        act.wait_ge(M["ht"], 1)
                        S.copy(hidT[:, 0:2, :], ps[5][:, 0:256].rearrange("p (j t) -> p j t", j=2)).then_inc(M["hta"], 1)
                        act.wait_ge(M["dn"], 1)
                        S.copy(ys[:, 0, 0:512], ps[3][:, :]).then_inc(M["ya"], 1)
                        act.wait_ge(M["ya"], 1)
                        act.wait_ge(M["yd"], 1)
                        act.dma_start(y_d[bass.ds(x * P + XROW, P), :], ys[:, 0, :]).then_inc(M["yst"], 16)
                        act.wait_ge(M["yst"], 16)
                        leave(act, "act")
                act.wait_ge(L["ready"], 1)
                for t in range(NT + 1):
                    if t < NT:
                        m = rows_of(t)
                        act.wait_ge(s_yg[t], (l + 1) * 32)
                        y1 = yg[0:m, 2 * t, :]
                        S.mul(y1, y1, route[0:m, R_G1 + t:R_G1 + t + 1]).then_inc(L["yg1"], 1)
                    if t >= 1:
                        act.wait_ge(L["comb"], t)
                        sum_of_squares(t - 1, (l + 1) * NT + t - 1)
                leave(act, "act")
            act.wait_ge(s_fin, 1)
            act.dma_start(O["y_prompt"].rearrange("b (t p) d -> p (b t) d", p=P), X[:, 0:4, :]).then_inc(y_out, 16)
            act.dma_start(O["y_sample"][0], X[0:DEC, 4, :]).then_inc(y_out, 16)
            act.wait_ge(y_out, 32)

        @block.vector
        def _(dve):
            V = nc.vector
            further = dve.alloc_register("dve_further")
            V.memset(small[:, :], 1.0).then_inc(s_init, 1)
            V.memset(zeros[:, :], 0.0).then_inc(s_init, 1)
            dve.sem_inc(s_adae, 2)
            dve.wait_ge(s_c, 16)
            V.tensor_copy(tokf[:, :], C[:, K_TOK:K_TOK + NT]).then_inc(s_init, 1)
            dve.wait_ge(s_cT, 1)
            V.tensor_copy(scT[:, :, :], ps[7][:, 0:16].rearrange("p (s k) -> p k s", s=2)).then_inc(s_cTc, 1)
            dve.wait_ge(s_b, 16)
            with dve.Fori(0, DEPTH) as l:
                with dve.Fori(0, 2) as h:
                    for u in range(2):
                        at = l * 6144 + h * 3072 + u * 1536
                        dve.wait_ge(s_ada, l * 4 + h * 2 + u + 1)
                        for c in range(3):
                            row = modr[0:2, bass.ds(at + 512 * c, 512)]
                            ins = V.tensor_tensor(row, ps[3 * u + c][0:2, :], row, ALU.add)
                        ins.then_inc(s_adae, 1)
            dve.wait_ge(s_init, 3)
            dve.wait_ge(s_x, 32)

            with dve.Fori(0, DEPTH) as l:
                n_chain = [0]

                def chain(ins):
                    n_chain[0] += 1
                    ins.then_inc(L["dch"], 1)
                    dve.wait_ge(L["dch"], n_chain[0])

                def inverse(sums, var, root, n, scale, s_in, n_in, s_var, s_root):
                    dve.wait_ge(s_in, n_in)
                    V.tensor_scalar(small[:, var:var + n], small[:, sums:sums + n], scale, EPS, ALU.mult, ALU.add).then_inc(s_var, 1)
                    dve.wait_ge(s_root, 1)
                    chain(V.reciprocal(small[:, root:root + n], small[:, root:root + n]))

                inverse(S_SS, S_VAR, S_RS, 5, 1.0 / D, s_sum, (l + 1) * NT, L["var"], L["root"])
                for t in range(NT):
                    m = rows_of(t)
                    V.tensor_scalar(XN[0:m, t, :], X[0:m, t, :], small[0:m, S_RS + t:S_RS + t + 1], None, ALU.mult).then_inc(L["xn"], 1)
                dve.wait_ge(L["vecT"], 2)
                V.tensor_copy(vT[:, :], ps[6][:, 0:52]).then_inc(L["vecC"], 1)
                cr = ps[7][:, 0:244].rearrange("p (c w) -> p c w", w=61)
                V.tensor_copy(taps[:, :, :], cr[:, :, 0:CW]).then_inc(L["vecC"], 1)
                V.tensor_copy(gT[:, :, 542:572], cr[:, :, CW:61]).then_inc(L["vecC"], 1)
                dve.wait_ge(L["vecC"], 3)
                V.scalar_tensor_tensor(small[:, S_AT:S_AT + 16].rearrange("p (s k) -> p s k", s=2),
                                       vT[:, 0:32].rearrange("p (s q k) -> p s q k", s=2, q=2)[:, :, 1, :], 1.0,
                                       vT[:, 32:40].unsqueeze(1).to_broadcast([P, 2, KC]), ALU.add, ALU.mult).then_inc(L["vecC"], 1)
                dve.wait_ge(L["vecC"], 4)
                for k in range(1, KC, 2):
                    dve.wait_ge(L["nT"], k + 1)
                    V.tensor_scalar(hT[:, k, 0:SEQ], ps[k][:, :], small[:, S_AT + k:S_AT + k + 1], vT[:, k:k + 1],
                                    ALU.mult, ALU.add).then_inc(L["nTd"], 1)
                dve.wait_ge(L["nT"], 10)
                for k in range(1, KC, 2):
                    V.tensor_scalar(hT[:, k, SEQ:TOK], ps[1][:, k * DEC:(k + 1) * DEC], small[:, S_AT + 8 + k:S_AT + 9 + k],
                                    vT[:, 16 + k:17 + k], ALU.mult, ALU.add).then_inc(L["nTd"], 1)

                taps_done = [0]
                dve.wait_ge(L["glup"], DVE_CONV)

                def conv(steps):
                    for _ in range(steps):
                        n = taps_done[0]
                        if n >= NCDVE:
                            return
                        w, c = divmod(n, DVE_CONV)
                        g = gT[:, c, w:w + 606]
                        if w == 0:
                            V.tensor_scalar(cy[:, c, :], g, taps[:, c, 0:1], vT[:, 40 + c:41 + c], ALU.mult, ALU.add).then_inc(L["cdve"], 1)
                        else:
                            dve.wait_ge(L["cdve"], n - DVE_CONV + 1)
                            V.scalar_tensor_tensor(cy[:, c, :], g, taps[:, c, w:w + 1], cy[:, c, :], ALU.mult, ALU.add).then_inc(L["cdve"], 1)
                        taps_done[0] += 1

                conv(74)
                dve.wait_ge(L["proja"], 10)
                for r, t0, t1 in PARTS:
                    rope(dve, V, iqr, r, t0, t1, 13424, L["dch"], n_chain, L["ropei"], 1 if t0 == 0 else 2)
                conv(8)

                for n, (t, h) in enumerate((t, h) for t in SCORED for h in range(8)):
                    m = rows_of(t)
                    sc = msk[0:m, MSK_AT[t]:MSK_AT[t] + NKEYS[t]]
                    dve.wait_ge(L["rel"], n + 1)
                    w = iw[0:m, t, h:h + 1]
                    if h == 0:
                        V.tensor_scalar(sc, rel[0:m, n % 3, 0:NKEYS[t]], w, None, ALU.mult).then_inc(L["score"], 1)
                    else:
                        dve.wait_ge(L["score"], n)
                        V.scalar_tensor_tensor(sc, rel[0:m, n % 3, 0:NKEYS[t]], w, sc, ALU.mult, ALU.add).then_inc(L["score"], 1)
                    conv(n % 2)
                dve.wait_ge(L["score"], 32)

                def select(t, a, b):
                    m, n = rows_of(t), NKEYS[t]
                    sc = msk[0:m, MSK_AT[t]:MSK_AT[t] + n]
                    m8 = small[0:m, S_M8:S_M8 + 8]
                    steps = TOPK[t] // 8
                    if t < 4 and a == 0:
                        chain(V.memset(sc[0:64, n - 64:n], -BIG))
                    for _ in range(int(steps * a), int(steps * b)):
                        chain(V.max(m8, sc))
                        chain(V.match_replace(sc, m8, sc, MARK))
                    if b == 1:
                        chain(V.tensor_scalar(sc, sc, MARK, -BIG, ALU.not_equal, ALU.mult))

                conv(NCDVE)
                select(4, 0, 1)
                select(3, 0, 0.75)
                dve.wait_ge(L["sqd"], NT)
                for r, t0, t1 in PARTS:
                    o = small[0:r, S_QS + 10 * t0:S_QS + 10 * t1]
                    chain(V.tensor_reduce(o.rearrange("p (t h) -> p t h", h=10), sq[0:r, t0:t1], AX.X, ALU.add))
                V.tensor_scalar(small[:, S_QS:S_QS + 50], small[:, S_QS:S_QS + 50], 1.0 / HD, EPS, ALU.mult, ALU.add).then_inc(L["qvar"], 1)
                dve.wait_ge(L["qroot"], 1)
                V.reciprocal(small[:, S_QS + 50:S_QS + 100], small[:, S_QS + 50:S_QS + 100]).then_inc(L["qinv"], 1)
                dve.wait_ge(L["lnm"], 2)
                dve.wait_ge(L["cdve"], NCDVE)
                for n, (b, a, w) in enumerate(((3, 0, SEQ), (4, 542, DEC))):
                    for c in range(4):
                        ins = V.scalar_tensor_tensor(cy[:, c, a:a + w], ps[b][:, 0:w], -1.0 / 512, cy[:, c, a:a + w], ALU.mult, ALU.add)
                    ins.then_inc(L["lnx"], 1)
                dve.wait_ge(L["qinv"], 1)
                norm_qk(V, chain, *PARTS[1])
                rope(dve, V, qkr, *PARTS[1], 15728, L["dch"], n_chain, L["ropes"], 1)
                select(3, 0.75, 1)
                dve.wait_ge(L["lnv"], 2)
                V.tensor_scalar(lnb[:, 0:SEQ], ps[5][:, :], 1.0 / 512, EPS, ALU.mult, ALU.add)
                V.tensor_scalar(lnb[:, SEQ:TOK], ps[6][:, 0:DEC], 1.0 / 512, EPS, ALU.mult, ALU.add).then_inc(L["lnr"], 1)
                dve.wait_ge(L["lnr"], 2)
                chain(V.reciprocal(lnb[:, :], lnb[:, :]))
                dve.wait_ge(L["lnx"], 2)
                for a, s, w in ((0, 0, SEQ), (542, SEQ, DEC)):
                    V.tensor_tensor(cy[:, :, a:a + w], cy[:, :, a:a + w], lnb[:, s:s + w].unsqueeze(1).to_broadcast([P, 4, w]),
                                    ALU.mult).then_inc(L["lny"], 1)

                def masked(n):
                    t, g = GROUPS[n]
                    m = rows_of(t)
                    mk = C[0:m, K_M0:K_M0 + P] if t == 0 else msk[0:m, MSK_AT[t]:MSK_AT[t] + NKEYS[t]]
                    if n >= 2:
                        dve.wait_ge(L["pt"], PT0[n - 2] + len(chunks_of(GROUPS[n - 2][0])))
                    for i in range(4):
                        job = 4 * n + i
                        dve.wait_ge(L["lgt"], job + 1)
                        r = PR[0:m, 4 * (n % 2) + i, :]
                        k = min(NKEYS[t], 512)
                        mx = S_MX + i
                        ins = V.tensor_tensor_reduce(r[:, 0:k], ps[logit_bank(job)][0:m, 0:k], mk[:, 0:k], 0.125, MARK, ALU.add, ALU.max,
                                                     small[0:m, mx:mx + 1])
                        if t == 4:
                            ins = V.tensor_tensor_reduce(r[:, 512:576], ps[2 + job % 2][0:m, 0:DEC], mk[:, 512:576], 0.125, MARK,
                                                         ALU.add, ALU.max, small[0:m, mx + 4:mx + 5])
                        ins.then_inc(L["ttr"], 1)
                    dve.wait_ge(L["ttr"], 4 * n + 4)
                    if t == 4:
                        chain(V.tensor_tensor(small[0:m, S_MX:S_MX + 4], small[0:m, S_MX:S_MX + 4], small[0:m, S_MX + 4:S_MX + 8], ALU.max))
                    if n >= 2:
                        dve.wait_ge(L["pexp"], n - 1)
                    q = S_NMX + 4 * (n % 2)
                    V.tensor_scalar(small[0:m, q:q + 4], small[0:m, S_MX:S_MX + 4], -1.0, None, ALU.mult).then_inc(L["nmx"], 1)
                    dve.wait_ge(L["nmx"], n + 1)

                dve.wait_ge(L["ropeq"], 1)
                dve.wait_ge(L["ropes"], 1)
                dve.wait_ge(L["outst"], 128)
                def inverses(n):
                    t, g = GROUPS[n]
                    m = rows_of(t)
                    s, q = S_SUM + 8 * ((n // 2) % 2) + 4 * g, S_INV + 4 * (n % 2)
                    dve.wait_ge(L["pexp"], n + 1)
                    if n >= 2:
                        dve.wait_ge(L["pn"], n - 1)
                    V.reciprocal(small[0:m, q:q + 4], small[0:m, s:s + 4]).then_inc(L["inv"], 1)

                masked(0)
                masked(1)
                inverses(0)
                for n in range(len(GROUPS)):
                    if n + 1 < len(GROUPS):
                        inverses(n + 1)
                    if n + 2 < len(GROUPS):
                        masked(n + 2)
                    if n < 4:
                        select(2 - n // 2, n % 2 / 2, n % 2 / 2 + 0.5)

                dve.wait_ge(L["gt_ld"], 32)
                for t in range(NT):
                    m = rows_of(t)
                    for hf in range(2):
                        n = 2 * t + hf
                        dve.wait_ge(L["wo"], n + 1)
                        if n >= 2:
                            dve.wait_ge(L["xadd"], n - 1)
                        V.tensor_tensor(wtmp[0:m, n % 2, :], ps[5 + n % 3][0:m, :], gt[0:m, t // 4, hf * 512:hf * 512 + 512],
                                        ALU.mult).then_inc(L["wod"], 1)
                    if t == 0:
                        dve.wait_ge(L["ab_ld"], 80)
                        for s, r in ((0, P), (1, DEC)):
                            chain(V.scalar_tensor_tensor(AB[s][0:r, 0, :], AB[s][0:r, 0, :], 1.0, gf[0:r, :], ALU.add, ALU.mult))
                    dve.wait_ge(L["fsum"], t + 1)
                    V.tensor_scalar(small[:, S_FV + t:S_FV + t + 1], small[:, S_FS + t:S_FS + t + 1], 1.0 / D, EPS, ALU.mult,
                                    ALU.add).then_inc(L["fvar"], 1)
                    dve.wait_ge(L["froot"], t + 1)
                    chain(V.reciprocal(small[:, S_FR + t:S_FR + t + 1], small[:, S_FR + t:S_FR + t + 1]))
                    if t >= 2:
                        dve.wait_ge(L[f"hst{t % 2}"], 16 * (t // 2))
                        dve.wait_ge(L["hTt"], 2 * (t - 1))
                    hr = HR[0:m, t % 2, :]
                    chain(V.scalar_tensor_tensor(hr, X[0:m, t, :], small[0:m, S_FR + t:S_FR + t + 1], AB[t // 4][0:m, 0, :], ALU.mult, ALU.mult))
                    V.tensor_tensor(hr, hr, AB[t // 4][0:m, 1, :], ALU.add).then_inc(L["hrow"], 1)

                def R(at, *shape):
                    n = int(np.prod(shape))
                    v = route[:, at:at + n]
                    return v.rearrange("p (t e) -> p t e", t=shape[0]) if len(shape) == 2 else v

                def wide(v, n):
                    return v.unsqueeze(2).to_broadcast([P, NT, n])

                def iota(n):
                    return C[:, K_E16:K_E16 + n].unsqueeze(1).to_broadcast([P, NT, n])

                def first_largest(v, n, big, eq, least, onehot):
                    chain(V.tensor_reduce(big, v, AX.X, ALU.max))
                    chain(V.tensor_tensor(eq, v, wide(big, n), ALU.is_equal))
                    chain(V.scalar_tensor_tensor(eq, eq, -100.0, iota(n), ALU.mult, ALU.add))
                    chain(V.tensor_reduce(least, eq, AX.X, ALU.min))
                    chain(V.tensor_tensor(onehot, eq, wide(least, n), ALU.is_equal))

                lg = R(R_LG, NT, 20)
                chain(V.memset(lg[64:128, 4, :], 0.0))
                dve.wait_ge(L["rl"], NT)
                for r, t0, t1 in PARTS:
                    chain(V.tensor_tensor(lg[0:r, t0:t1], ps[4][0:r, t0 * 20:t1 * 20].rearrange("p (t e) -> p t e", e=20),
                                          rb[0:r, :].unsqueeze(1).to_broadcast([r, t1 - t0, 20]), ALU.add))
                goh, em = R(R_GOH, NT, 4), R(R_EM, NT, NE)
                oh1, oh2 = R(R_OH1, NT, NE), R(R_OH2, NT, NE)
                first_largest(lg[:, :, 0:4], 4, R(R_GM, NT), R(R_EQ, NT, 4), R(R_MI, NT), goh)
                V.tensor_tensor(R(R_GE, NT, 4), lg[:, :, 0:4], wide(R(R_GM, NT), 4), ALU.subtract).then_inc(L["gdiff"], 1)
                chain(V.tensor_scalar(R(R_W, NT, 4), goh, 1.0, BIG, ALU.subtract, ALU.mult))
                for g in range(4):
                    V.tensor_tensor(em[:, :, 4 * g:4 * g + 4], lg[:, :, 4 + 4 * g:8 + 4 * g],
                                    wide(R(R_W, NT, 4)[:, :, g], 4), ALU.add)
                chain(V.memset(R(R_TMP, NT, NE), 0.0))
                chain(V.tensor_scalar(em, em, 1.0, None, ALU.mult))
                first_largest(em, NE, R(R_M1, NT), R(R_EQ1, NT, NE), R(R_MI1, NT), oh1)
                chain(V.scalar_tensor_tensor(em, oh1, -BIG, em, ALU.mult, ALU.add))
                first_largest(em, NE, R(R_M2, NT), R(R_EQ1, NT, NE), R(R_MI1, NT), oh2)
                V.tensor_tensor(R(R_Z, NT), R(R_M2, NT), R(R_M1, NT), ALU.subtract).then_inc(L["zdiff"], 1)
                chain(V.memset(oh1[64:128, 4, :], 0.0))
                chain(V.memset(oh2[64:128, 4, :], 0.0))
                V.tensor_tensor(R(R_AS, NT, NE), oh1, oh2, ALU.add).then_inc(L["assign"], 1)
                dve.wait_ge(L["gexp"], 1)
                chain(V.tensor_reduce(R(R_PG, NT), R(R_GE, NT, 4), AX.X, ALU.add))
                dve.wait_ge(L["zexp"], 1)
                chain(V.tensor_scalar(R(R_G2, NT), R(R_Z, NT), 1.0, None, ALU.add))
                chain(V.tensor_tensor(R(R_G1, NT), R(R_G2, NT), R(R_PG, NT), ALU.mult))
                chain(V.reciprocal(R(R_G1, NT), R(R_G1, NT)))
                chain(V.tensor_tensor(R(R_G2, NT), R(R_G1, NT), R(R_Z, NT), ALU.mult))
                dve.wait_ge(L["pos"], 1)
                dve.wait_ge(L["assign"], 1)
                place, upto = R(R_PL, NT, NE), R(R_UP, NT, NE)
                counts = ps[5][:, 80:160].rearrange("p (t e) -> p t e", e=NE)
                V.tensor_copy(place[:, 0, :], ps[5][:, 0:NE])
                chain(V.tensor_copy(upto[:, 0, :], counts[:, 0, :]))
                for t in range(1, NT):
                    chain(V.tensor_tensor(upto[:, t, :], upto[:, t - 1, :], counts[:, t, :], ALU.add))
                chain(V.tensor_tensor(place[:, 1:NT, :], ps[5][:, NE:80].rearrange("p (t e) -> p t e", e=NE), upto[:, 0:NT - 1, :], ALU.add))
                pos, tmp = R(R_POS, NT, NE), R(R_TMP, NT, NE)
                chain(V.scalar_tensor_tensor(pos, place, 1.0, R(R_AS, NT, NE), ALU.add, ALU.mult))
                chain(V.tensor_scalar(pos, pos, -1.0, None, ALU.add))

                for t in range(NT):
                    if t >= 2:
                        dve.wait_ge(L["ohu"], t - 1)
                    V.tensor_tensor(oh[:, t % 2], C[:, K_IOTA:K_IOTA + P].unsqueeze(1).to_broadcast([P, NE, P]),
                                    pos[:, t, :].unsqueeze(2).to_broadcast([P, NE, P]), ALU.is_equal).then_inc(L["oh"], 1)
                dve.wait_ge(L["ohu"], NT)
                V.tensor_copy(idx[:, 0:NE], ps[6][:, 0:NE]).then_inc(L["idx"], 1)

                exceeds = R(R_XC, 4 * NE).rearrange("p (q e) -> p q e", e=NE)
                for q in range(4):
                    ins = V.tensor_scalar(exceeds[:, q, :], upto[:, NT - 1, :], P * (q + 1.0), None, ALU.is_gt)
                chain(ins)
                sums = R(R_EM, 3 * NE)
                own, odd, even = sums[:, 0:NE], sums[:, NE:2 * NE], sums[:, 2 * NE:3 * NE]
                chain(V.tensor_reduce(own, exceeds.rearrange("p q e -> p e q"), AX.X, ALU.add))
                src = own
                for n, d in enumerate((1, 2, 4, 8)):
                    dst = odd if n % 2 == 0 else even
                    V.tensor_copy(dst[:, 0:d], src[:, 0:d])
                    chain(V.tensor_tensor(dst[:, d:NE], src[:, d:NE], src[:, 0:NE - d], ALU.add))
                    src = dst
                incl = src
                before = R(R_RT, XJ * NE).rearrange("p (j e) -> p j e", e=NE)
                expert = R(R_LG, XJ + 1)
                chain(V.tensor_tensor(before, incl.unsqueeze(1).to_broadcast([P, XJ, NE]),
                                      C[:, K_E16:K_E16 + XJ].unsqueeze(2).to_broadcast([P, XJ, NE]), ALU.is_le))
                V.tensor_reduce(expert[:, 0:XJ], before, AX.X, ALU.add)
                chain(V.tensor_copy(expert[:, XJ:XJ + 1], incl[:, NE - 1:NE]))
                V.tensor_copy(jobs[:, :], expert).then_inc(L["dch"], 1)
                n_chain[0] += 1
                rt = R(R_RT, NT, NE)
                chain(V.tensor_tensor(own, incl, own, ALU.subtract))
                chain(V.tensor_scalar(own, own, float(P), float(XROW - P), ALU.mult, ALU.add))
                chain(V.tensor_tensor(own, own, C[:, K_ROW:K_ROW + NE], ALU.subtract))
                chain(V.scalar_tensor_tensor(tmp, place, P - 0.5, own.unsqueeze(1).to_broadcast([P, NT, NE]), ALU.is_gt, ALU.mult))
                chain(V.tensor_tensor(tmp, tmp, place, ALU.add))
                chain(V.tensor_tensor(tmp, tmp, C[:, K_ROW:K_ROW + NE].unsqueeze(1).to_broadcast([P, NT, NE]), ALU.add))
                for k, o in enumerate((oh1, oh2)):
                    chain(V.tensor_tensor(rt, tmp, o, ALU.mult))
                    chain(V.tensor_reduce(R(R_S + 5 * k, NT), rt, AX.X, ALU.add))
                chain(V.tensor_copy(sid[:, :], R(R_S, 2 * NT)))
                dve.sem_inc(n_cnt, 1)
                dve.sem_inc(L["ready"], 1)


                def turned_x(e, u):
                    dve.wait_ge(L["tx"], e * 2 + 2)
                    V.tensor_copy(xgT[:, u * KC + 4:u * KC + 8, :], ps[1][:, :].rearrange("p (j t) -> p j t", j=4)).then_inc(L["txd"], 1)

                def y_half(e, u):
                    dve.wait_ge(L["dn"], e * 2 + 2)
                    V.tensor_copy(ys[:, u, 512:1024], ps[4][:, :]).then_inc(L["yd"], 1)

                def step(i, u, head, tail):
                    e = i * 2 + u
                    dve.wait_ge(L["sg"], e + 1)
                    V.tensor_tensor(hid[:, u, :], sg[:, u, :], ps[2][:, DE:2 * DE], ALU.mult).then_inc(L["hid"], 1)
                    if not (tail and u == 1):
                        turned_x(e + 1, 1 - u)
                    if not (head and u == 0):
                        if not head and not (isinstance(i, int) and i - 1 + u == 0):
                            dve.wait_ge(L[f"yst{1 - u}"], (i - 1 + u) * 16)
                        y_half(e - 1, 1 - u)

                turned_x(0, 0)
                for u in range(2):
                    step(0, u, True, False)
                for u in range(2):
                    step(1, u, False, False)
                with dve.Fori(2, NE // 2 - 1) as i:
                    for u in range(2):
                        step(i, u, False, False)
                for u in range(2):
                    step(NE // 2 - 1, u, False, True)
                dve.wait_ge(L["yst1"], 16 * (NE // 2 - 1))
                y_half(NE - 1, 1)
                xrow = R(R_TMP, 2 * NT)
                chain(V.tensor_scalar(xrow, R(R_S, 2 * NT), -float(XROW), None, ALU.add))
                dve.reg_load(further, jobs[0:1, XJ:XJ + 1])
                with dve.If_ne(further, 0):
                    with dve.Fori(0, dve.snap(further, min_val=0, max_val=XJ)):
                        V.tensor_tensor(ohx[:, :, :], C[:, K_IOTA:K_IOTA + P].unsqueeze(1).to_broadcast([P, 2 * NT, P]),
                                        xrow.unsqueeze(2).to_broadcast([P, 2 * NT, P]), ALU.is_equal).then_inc(M["oh"], 1)
                        dve.wait_ge(M["idx"], 1)
                        V.tensor_copy(idx[:, NE:NE + 1], ps[6][:, 0:1]).then_inc(M["idc"], 1)
                        dve.wait_ge(M["tx"], 2)
                        V.tensor_copy(xgT[:, 4:8, :], ps[1][:, :].rearrange("p (j t) -> p j t", j=4)).then_inc(M["txd"], 1)
                        dve.wait_ge(M["sg"], 1)
                        V.tensor_tensor(hid[:, 0, :], sg[:, 0, :], ps[2][:, DE:2 * DE], ALU.mult).then_inc(M["hid"], 1)
                        dve.wait_ge(M["dn"], 2)
                        dve.wait_ge(L["yst0"], 16 * (NE // 2))
                        V.tensor_copy(ys[:, 0, 512:1024], ps[4][:, :]).then_inc(M["yd"], 1)
                        dve.wait_ge(M["oh"], 1)
                        V.tensor_scalar(xrow, xrow, -float(P), None, ALU.add).then_inc(M["rch"], 1)
                        dve.wait_ge(M["rch"], 1)
                        release(dve, mrange)

                dve.wait_ge(L["gtf_ld"], 32)
                for t in range(NT):
                    m = rows_of(t)
                    dve.wait_ge(s_yg[t], (l + 1) * 32)
                    y1, y2 = yg[0:m, 2 * t, :], yg[0:m, 2 * t + 1, :]
                    dve.wait_ge(L["yg1"], t + 1)
                    chain(V.scalar_tensor_tensor(y1, y2, route[0:m, R_G2 + t:R_G2 + t + 1], y1, ALU.mult, ALU.add))
                    V.tensor_tensor(y1, y1, gt[0:m, t // 4, :], ALU.mult).then_inc(L["ygt"], 1)
                release(dve, lrange)
            dve.sem_inc(s_fin, 1)

        @block.gpsimd
        def _(pool):
            G = nc.gpsimd
            further = pool.alloc_register("pool_further")
            with pool.Fori(0, DEPTH) as l:
                n_chain = [0]

                def chain(ins):
                    n_chain[0] += 1
                    ins.then_inc(L["pch"], 1)
                    pool.wait_ge(L["pch"], n_chain[0])

                pool.wait_ge(s_mst, 16)
                chain(G.memset(gT[:, :, 0:30], 0.0))

                def multiply(i):
                    pool.wait_ge(L["glua"], i + 1)
                    s = 2 * (i % 2)
                    G.tensor_tensor(gT[:, i, 30:542], glu[:, s, 0:SEQ], glu[:, s + 1, 0:SEQ], ALU.mult)
                    G.tensor_tensor(gT[:, i, 572:636], glu[:, s, SEQ:TOK], glu[:, s + 1, SEQ:TOK], ALU.mult).then_inc(L["glup"], 1)
                for i in range(4):
                    multiply(i)
                pool.wait_ge(L["glup"], 4)
                pool.wait_ge(L["vecC"], 4)
                for w in range(CW):
                    for c in range(DVE_CONV, 4):
                        g = gT[:, c, w:w + 606]
                        if w == 0:
                            G.tensor_scalar(cy[:, c, :], g, taps[:, c, 0:1], vT[:, 40 + c:41 + c], ALU.mult, ALU.add).then_inc(L["cpool"], 1)
                        else:
                            n = w * (4 - DVE_CONV) + c - DVE_CONV
                            pool.wait_ge(L["cpool"], max(n - 1, 1))
                            chain(G.tensor_scalar(ctmp[:, n % 2, :], g, taps[:, c, w:w + 1], None, ALU.mult))
                            pool.wait_ge(L["cpool"], n - 4 + DVE_CONV + 1)
                            G.tensor_tensor(cy[:, c, :], cy[:, c, :], ctmp[:, n % 2, :], ALU.add).then_inc(L["cpool"], 1)
                pool.wait_ge(L["qinv"], 1)
                pool.wait_ge(L["outst"], 96)
                norm_qk(G, chain, *PARTS[0])
                rope(pool, G, qkr, *PARTS[0], 19760, L["pch"], n_chain, L["ropeq"], 1)
                for n, (t, g) in enumerate(GROUPS):
                    m = rows_of(t)
                    pool.wait_ge(L["inv"], n + 1)
                    for i in range(4):
                        h = S_INV + 4 * (n % 2) + i
                        r = PR[0:m, 4 * (n % 2) + i, 0:NKEYS[t]]
                        ins = G.tensor_scalar(r, r, small[0:m, h:h + 1], None, ALU.mult)
                    ins.then_inc(L["pn"], 1)
                for n in range(10):
                    t, hf = n // 2, n % 2
                    m = rows_of(t)
                    pool.wait_ge(L["wod"], n + 1)
                    xs = X[0:m, t, hf * 512:hf * 512 + 512]
                    G.tensor_tensor(xs, xs, wtmp[0:m, n % 2, :], ALU.add).then_inc(L["xadd"], 1)
                pool.wait_ge(L["hst0"], 48)
                pool.wait_ge(L["hst1"], 32)
                pool.wait_ge(L["idx"], 1)
                for e in range(NE):
                    if e >= 2:
                        pool.wait_ge(L["tx"], 2 * (e - 1))
                    G.indirect_dma_start(out=xg[:, e % 2, :], out_offset=None, in_=h_d[:, :],
                                         in_offset=bass.IndirectOffsetOnAxis(ap=idx[:, e:e + 1], axis=0)).then_inc(s_xg[e % 2], 16)
                pool.wait_ge(L["tx"], 2 * NE)
                pool.wait_ge(L["ready"], 1)
                pool.reg_load(further, jobs[0:1, XJ:XJ + 1])
                with pool.If_ne(further, 0):
                    with pool.Fori(0, pool.snap(further, min_val=0, max_val=XJ)):
                        pool.wait_ge(M["idc"], 1)
                        G.indirect_dma_start(out=xg[:, 0, :], out_offset=None, in_=h_d[:, :],
                                             in_offset=bass.IndirectOffsetOnAxis(ap=idx[:, NE:NE + 1], axis=0)).then_inc(s_xx, 16)
                        leave(pool, "pool")
                pool.wait_ge(L["yst0"], 16 * (NE // 2))
                pool.wait_ge(L["yst1"], 16 * (NE // 2))
                pool.wait_ge(L["zst"], 16)
                for t in range(NT):
                    m = rows_of(t)
                    for k in range(2):
                        G.indirect_dma_start(out=yg[0:m, 2 * t + k, :], out_offset=None, in_=y_d[:, :],
                                             in_offset=bass.IndirectOffsetOnAxis(ap=sid[0:m, 5 * k + t:5 * k + t + 1], axis=0)
                                             ).then_inc(s_yg[t], 16)
                for t in range(NT):
                    m = rows_of(t)
                    pool.wait_ge(L["ygt"], t + 1)
                    G.tensor_tensor(X[0:m, t, :], X[0:m, t, :], yg[0:m, 2 * t, :], ALU.add).then_inc(L["comb"], 1)
                leave(pool, "pool")


_INS = ["x_prompt", "x_sample", "c_prompt", "c_sample", "cache_k", "cache_v", "cache_idx_k", "state_conv",
        "w_ada", "b_ada", "g_norm_mix", "w_in", "q_norm_g", "k_norm_g", "conv_w", "conv_b", "ln_conv_g", "ln_conv_b",
        "w_out", "g_norm_ffn", "w_router_group", "b_router_group", "w_router_expert", "b_router_expert",
        "w_gate", "w_up", "w_down"]
_OUTS = [("y_prompt", (1, SEQ, D)), ("y_sample", (1, DEC, D)),
         ("new_k_prompt", (DEPTH, 1, SEQ, 2, HD)), ("new_v_prompt", (DEPTH, 1, SEQ, 2, HD)),
         ("new_idx_k_prompt", (DEPTH, 1, SEQ, HD)), ("new_conv_prompt", (DEPTH, 1, CW - 1, 512)),
         ("new_k_sample", (DEPTH, 1, DEC, 2, HD)), ("new_v_sample", (DEPTH, 1, DEC, 2, HD)),
         ("new_idx_k_sample", (DEPTH, 1, DEC, HD)), ("new_conv_sample", (DEPTH, 1, CW - 1, 512))]


def kernel(**inputs):
    import concourse.bacc as _bacc
    from concourse.bass_utils import run_bass_kernel_spmd as _run

    nc = _bacc.Bacc("TRN2", target_bir_lowering=False, num_devices=1)
    arrays, ins, outs = {}, {}, {}
    for name in _INS:
        a = np.ascontiguousarray(inputs[name])
        arrays[f"in_{name}"] = a
        ins[name] = nc.dram_tensor(f"in_{name}", a.shape, F32, kind="ExternalInput").ap()
    arrays["in_consts"] = constants()
    ins["consts"] = nc.dram_tensor("in_consts", (P, NCONST), F32, kind="ExternalInput").ap()
    for name, shape in _OUTS:
        outs[name] = nc.dram_tensor(f"out_{name}", shape, F32, kind="ExternalOutput").ap()
    program(nc, ins, outs)
    r = _run(nc, [arrays], core_ids=[0])
    return tuple(r.results[0][f"out_{name}"] for name, _ in _OUTS)
```
